# Optimizing a Trainium2 kernel written in Bass

```python
import math
import jax, jax.numpy as jnp
from jax import lax
import numpy as np

D_MODEL = 1024
BATCH = 1
SEQ = 512
DEPTH = 1

MEM_LEN = 256
RMS_EPS = 1e-6

SB_HEADS = 16
SB_HEAD_DIM = 64
SB_WIDTH = SB_HEADS * SB_HEAD_DIM
SB_BLOCK = 128

CONV_WIDTH = D_MODEL
CONV_K = 3

IN_COLS = 3 * SB_WIDTH + 3 * CONV_WIDTH + 2 * D_MODEL
IN_SPLITS = (SB_WIDTH, 2 * SB_WIDTH, 3 * SB_WIDTH,
             3 * SB_WIDTH + CONV_WIDTH, 3 * SB_WIDTH + 2 * CONV_WIDTH, 3 * SB_WIDTH + 3 * CONV_WIDTH,
             3 * SB_WIDTH + 3 * CONV_WIDTH + D_MODEL)

XATTN_HEADS = 4
XATTN_HEAD_DIM = D_MODEL // XATTN_HEADS

PEER_HEADS = 8
PEER_N_KEYS = 128
PEER_N_EXPERTS = PEER_N_KEYS * PEER_N_KEYS
PEER_KEY_DIM = 256
PEER_HALF = PEER_KEY_DIM // 2
PEER_TOPK = 16
PEER_TOKEN_CHUNK = 128

kernel_name = "hybrid_sb_shortconv_xmem_peer"

def rmsnorm(x, g):
    xf = x.astype(jnp.float32)
    y = xf * lax.rsqrt(jnp.mean(xf * xf, axis=-1, keepdims=True) + RMS_EPS) * g.astype(jnp.float32)
    return y.astype(x.dtype)

def stick_breaking_attention(q, k, v):
    s = q.shape[2]
    scale = 1.0 / math.sqrt(q.shape[-1])
    outs = []
    for blk in range(s // SB_BLOCK):
        start = blk * SB_BLOCK
        end = start + SB_BLOCK
        z = jnp.einsum('bhqd,bhkd->bhqk', q[:, :, start:end], k[:, :, :end]).astype(jnp.float32) * scale
        t_idx = start + jnp.arange(SB_BLOCK)[:, None]
        s_idx = jnp.arange(end)[None, :]
        causal = s_idx < t_idx
        log_stay = jnp.where(causal, jax.nn.log_sigmoid(-z), 0.0)
        log_after = lax.cumsum(log_stay, axis=3, reverse=True) - log_stay
        w = jnp.where(causal, jnp.exp(jax.nn.log_sigmoid(z) + log_after), 0.0)
        outs.append(jnp.einsum('bhqk,bhkd->bhqd', w.astype(v.dtype), v[:, :, :end]))
    return jnp.concatenate(outs, axis=2)

def causal_short_conv(u, w):
    s = u.shape[1]
    padded = jnp.pad(u, ((0, 0), (CONV_K - 1, 0), (0, 0)))
    y = padded[:, 0:s] * w[0]
    for i in range(1, CONV_K):
        y = y + padded[:, i:i + s] * w[i]
    return y

def memory_cross_attention(xn, memn, wq, wk, wv, wo):
    b, s, _ = xn.shape
    m = memn.shape[1]
    q = (xn @ wq).reshape(b, s, XATTN_HEADS, XATTN_HEAD_DIM)
    k = (memn @ wk).reshape(b, m, XATTN_HEADS, XATTN_HEAD_DIM)
    v = (memn @ wv).reshape(b, m, XATTN_HEADS, XATTN_HEAD_DIM)
    scores = jnp.einsum('bshd,bmhd->bhsm', q, k).astype(jnp.float32) / math.sqrt(XATTN_HEAD_DIM)
    p = jax.nn.softmax(scores, axis=-1).astype(v.dtype)
    o = jnp.einsum('bhsm,bmhd->bshd', p, v).reshape(b, s, XATTN_HEADS * XATTN_HEAD_DIM)
    return o @ wo

def peer_ffn(xn, w_query, sub_keys, expert_u, expert_v):
    b, s, d = xn.shape
    q = (xn @ w_query).reshape(b, s, PEER_HEADS, 2, PEER_HALF).astype(jnp.float32)
    sc = jnp.einsum('bshcd,hcnd->bshcn', q, sub_keys.astype(jnp.float32))
    top_s, top_i = lax.top_k(sc, PEER_TOPK)
    cand_s = top_s[..., 0, :, None] + top_s[..., 1, None, :]
    cand_i = top_i[..., 0, :, None] * PEER_N_KEYS + top_i[..., 1, None, :]
    cand_s = cand_s.reshape(b, s, PEER_HEADS, PEER_TOPK * PEER_TOPK)
    cand_i = cand_i.reshape(b, s, PEER_HEADS, PEER_TOPK * PEER_TOPK)
    best_s, best_pos = lax.top_k(cand_s, PEER_TOPK)
    expert_idx = jnp.take_along_axis(cand_i, best_pos, axis=-1)
    gates = jax.nn.softmax(best_s, axis=-1)

    n_tok = b * s
    n_chunks = n_tok // PEER_TOKEN_CHUNK
    n_sel = PEER_HEADS * PEER_TOPK
    xc = xn.reshape(n_chunks, PEER_TOKEN_CHUNK, d)
    ic = expert_idx.reshape(n_chunks, PEER_TOKEN_CHUNK, n_sel)
    gc = gates.reshape(n_chunks, PEER_TOKEN_CHUNK, n_sel).astype(xn.dtype)

    def chunk_fn(args):
        xb, ib, gb = args
        u = expert_u[ib]
        act = jax.nn.gelu(jnp.einsum('ced,cd->ce', u, xb))
        return jnp.einsum('ce,ced->cd', gb * act, expert_v[ib])

    out = lax.map(chunk_fn, (xc, ic, gc))
    return out.reshape(b, s, d)

def setup_inputs(seed: int = 0) -> dict:
    key = jax.random.key(seed)
    ks = jax.random.split(key, 24)

    def w(k, shape, fan_in):
        return jax.random.normal(k, shape, jnp.float32) * (fan_in ** -0.5)

    def gain(k, shape):
        return 1.0 + 0.02 * jax.random.normal(k, shape, jnp.float32)

    L = DEPTH
    return {
        "x": jax.random.normal(ks[0], (BATCH, SEQ, D_MODEL), jnp.float32),
        "mem": jax.random.normal(ks[1], (BATCH, MEM_LEN, D_MODEL), jnp.float32),
        "norm_mix": gain(ks[2], (L, D_MODEL)),
        "w_in": w(ks[3], (L, D_MODEL, IN_COLS), D_MODEL),
        "conv_w": w(ks[4], (L, CONV_K, CONV_WIDTH), CONV_K),
        "w_branch_attn": w(ks[5], (L, SB_WIDTH, D_MODEL), SB_WIDTH),
        "w_branch_conv": w(ks[6], (L, CONV_WIDTH, D_MODEL), CONV_WIDTH),
        "w_out": w(ks[7], (L, D_MODEL, D_MODEL), D_MODEL),
        "norm_xattn": gain(ks[8], (L, D_MODEL)),
        "norm_mem": gain(ks[9], (L, D_MODEL)),
        "xattn_wq": w(ks[10], (L, D_MODEL, XATTN_HEADS * XATTN_HEAD_DIM), D_MODEL),
        "xattn_wk": w(ks[11], (L, D_MODEL, XATTN_HEADS * XATTN_HEAD_DIM), D_MODEL),
        "xattn_wv": w(ks[12], (L, D_MODEL, XATTN_HEADS * XATTN_HEAD_DIM), D_MODEL),
        "xattn_wo": w(ks[13], (L, XATTN_HEADS * XATTN_HEAD_DIM, D_MODEL), XATTN_HEADS * XATTN_HEAD_DIM),
        "norm_ffn": gain(ks[14], (L, D_MODEL)),
        "peer_w_query": w(ks[15], (L, D_MODEL, PEER_HEADS * PEER_KEY_DIM), D_MODEL),
        "peer_sub_keys": w(ks[16], (L, PEER_HEADS, 2, PEER_N_KEYS, PEER_HALF), PEER_HALF),
        "peer_u": w(ks[17], (L, PEER_N_EXPERTS, D_MODEL), D_MODEL),
        "peer_v": w(ks[18], (L, PEER_N_EXPERTS, D_MODEL), PEER_HEADS),
        "norm_final": gain(ks[19], (D_MODEL,)),
    }

def reference(x, mem, norm_mix, w_in, conv_w, w_branch_attn, w_branch_conv, w_out,
              norm_xattn, norm_mem, xattn_wq, xattn_wk, xattn_wv, xattn_wo,
              norm_ffn, peer_w_query, peer_sub_keys, peer_u, peer_v, norm_final):
    b, s, _ = x.shape
    h = x
    for l in range(DEPTH):
        xn = rmsnorm(h, norm_mix[l])
        proj = xn @ w_in[l]
        q, k, v, cx, cb, cc, ga, gcv = jnp.split(proj, IN_SPLITS, axis=-1)

        def heads(t):
            return t.reshape(b, s, SB_HEADS, SB_HEAD_DIM).transpose(0, 2, 1, 3)

        y_attn = stick_breaking_attention(heads(q), heads(k), heads(v))
        y_attn = y_attn.transpose(0, 2, 1, 3).reshape(b, s, SB_WIDTH)
        y_conv = cb * causal_short_conv(cc * cx, conv_w[l])
        merged = (jax.nn.sigmoid(ga) * (y_attn @ w_branch_attn[l])
                  + jax.nn.sigmoid(gcv) * (y_conv @ w_branch_conv[l]))
        h = h + merged @ w_out[l]

        xn = rmsnorm(h, norm_xattn[l])
        memn = rmsnorm(mem, norm_mem[l])
        h = h + memory_cross_attention(xn, memn, xattn_wq[l], xattn_wk[l], xattn_wv[l], xattn_wo[l])

        xn = rmsnorm(h, norm_ffn[l])
        h = h + peer_ffn(xn, peer_w_query[l], peer_sub_keys[l], peer_u[l], peer_v[l])
    return rmsnorm(h, norm_final)


_drawn_inputs = setup_inputs


def setup_inputs(seed=0):
    import zlib

    import numpy as np

    out = dict(_drawn_inputs(seed))
    spreads = {}
    factors = {'norm_xattn': 8.0, 'norm_mem': 6.338, 'norm_final': 8.047, 'norm_ffn': 8.0}
    for name, (base, spread) in spreads.items():
        noise = np.random.default_rng([zlib.crc32(name.encode()), seed]).standard_normal(out[name].shape)
        drawn = base * np.exp(spread * noise) if base else spread * noise
        out[name] = __import__('jax').numpy.asarray(drawn.astype(out[name].dtype))
    for name, factor in factors.items():
        out[name] = (out[name] * factor).astype(out[name].dtype)
    return out
```

```python
from contextlib import ExitStack

import concourse.bass as bass
from concourse import mybir

F32 = mybir.dt.float32
U32 = mybir.dt.uint32
ALU = mybir.AluOpType
ACT = mybir.ActivationFunctionType
AX = mybir.AxisListType

P = 128
BANK = 512
BANKS = 4
RING = 8
EPS = 1e-6
SP_CAP = 40.0
GELU_C = 2.0 * 0.7978845608028654
GELU_FLOOR = -50.0
LOWEST = -3.0e38


def build_trunk(nc, x, mem, norm_mix, w_in, conv_w, w_branch_attn, w_branch_conv, w_out,
                norm_xattn, norm_mem, xattn_wq, xattn_wk, xattn_wv, xattn_wo,
                norm_ffn, peer_w_query, peer_sub_keys, peer_u, peer_v, norm_final, out):
    D = x.shape[2]
    SEQ = x.shape[1]
    M = mem.shape[1]
    KT = D // P
    TT = SEQ // P
    MT = M // P
    SBH, DH = 16, 64
    XH, XD = 4, D // 4
    PH, NK, TOPK = peer_sub_keys.shape[1], peer_sub_keys.shape[3], 16
    CONVK = conv_w.shape[1]
    NROW = 3 * KT + CONVK * KT
    GROUPS = TT * PH
    PAIRS = GROUPS // 2
    assert SBH * DH == D and (KT, TT, MT, NK, TOPK, PH) == (8, 4, 2, 128, 16, 8)

    WID = [SEQ - P * j for j in range(TT)]
    OFF = [0, BANK, 2 * BANK, 2 * BANK + WID[2]]
    SPAN = OFF[3] + WID[3]

    COLQ, COLK, COLV, COLX, COLB, COLC, COLGA, COLGC = (KT * n for n in range(8))

    J_PARAM = 0
    J_NORM1 = J_PARAM + 1
    J_KEYS = J_NORM1 + 2 * TT
    J_QK = J_KEYS + 4
    J_V = J_QK + 2 * KT
    J_MIX = J_V + 2 * TT
    J_WC = J_MIX + 4 * KT
    J_GA = J_WC + KT
    J_WO = J_GA + 2 * KT
    J_MEMT = J_WO + 2 * TT
    J_XK = J_MEMT + 2 * MT
    J_XV = J_XK + KT
    J_NORM2 = J_XV + 2 * MT
    J_XQ = J_NORM2 + 2 * TT
    J_SP = J_XQ + KT
    J_O = J_SP + 4 * TT
    J_XO = J_O + KT
    J_NORM3 = J_XO + 2 * TT
    NQ = 2 * PH
    J_PQ = J_NORM3 + 2 * TT
    J_PQR = J_PQ + 2 * NQ
    REST = SEQ - P

    def job_s(i):
        return J_SP + (4 * i - 2 if i else 0)

    def job_p(i):
        return J_SP + (4 * i + 4 if i < TT - 1 else 4 * TT - 2)

    def job_f(c):
        return J_PQ + (2 * c - 1 if c else 0)

    def job_k(c):
        return J_PQ + (2 * c + 2 if c < NQ - 1 else 2 * NQ - 1)

    def job_fr(c):
        return J_PQR + 2 * (c - c % 2) + c % 2

    def job_kr(c):
        return job_fr(c) + 2

    def plain(w2, col, job):
        return [(w2, col + s, job + s) for s in range(RING)]

    def by_tokens(w2, col, job, tiles):
        return [(w2, col + s, job + tiles * (s // 4) + tiles - 1) for s in range(RING)]

    w_in2, wa2 = w_in[0], w_branch_attn[0]
    blocks = [plain(w_in2, COLQ, J_QK), plain(w_in2, COLK, J_QK + KT), by_tokens(w_in2, COLV, J_V, TT)]
    B_MIX = len(blocks)
    for m in range(0, KT, 2):
        blocks.append([(w_in2, (COLX, COLC, COLB, COLGC)[s % 4] + m + s // 4, J_MIX + 4 * m + s) for s in range(RING)])
    B_WC = len(blocks)
    blocks.append(plain(w_branch_conv[0], 0, J_WC))
    B_GA = len(blocks)
    for m in range(0, KT, 4):
        blocks.append([((w_in2, COLGA) if s % 2 == 0 else (wa2, 0)) for s in range(RING)])
        blocks[-1] = [(w2, c0 + m + s // 2, J_GA + 2 * m + s) for s, (w2, c0) in enumerate(blocks[-1])]
    B_WO = len(blocks)
    blocks.append(by_tokens(w_out[0], 0, J_WO, TT))
    B_XK = len(blocks)
    blocks.append(plain(xattn_wk[0], 0, J_XK))
    B_XV = len(blocks)
    blocks.append(by_tokens(xattn_wv[0], 0, J_XV, MT))
    B_XQ = len(blocks)
    blocks.append(plain(xattn_wq[0], 0, J_XQ))
    B_XO = len(blocks)
    blocks.append(by_tokens(xattn_wo[0], 0, J_XO, TT))
    B_PQ = len(blocks)
    for c in range(0, NQ, RING):
        blocks.append([(peer_w_query[0], c + s, job_f(c + s)) for s in range(RING)])
    B_PQR = len(blocks)
    for c in range(0, NQ, RING):
        blocks.append([(peer_w_query[0], c + s, job_fr(c + s)) for s in range(RING)])

    with ExitStack() as ctx:
        def sb(name, shape, dt=F32):
            return ctx.enter_context(nc.sbuf_tensor(name, shape, dt))

        def sem(name):
            return ctx.enter_context(nc.semaphore(name))

        xT = sb("xT", [P, KT, SEQ])
        qk = sb("qk", [P, 2 * KT, SEQ])
        vbuf = sb("vbuf", [P, TT, D])
        h = sb("h", [P, TT, D])
        ymix = sb("ymix", [P, 2 * KT, SEQ])
        wring = sb("wring", [P, RING, KT, P])
        memkv = sb("memkv", [P, 4, D])
        keysT = sb("keysT", [P, NQ, NK])
        workf = sb("workf", [P, 9 * BANK])
        ident = sb("ident", [P, P])
        tri = sb("tri", [P, P])
        ones = sb("ones", [P, P])
        cmask = sb("cmask", [P, P])
        nmask = sb("nmask", [P, P])
        rows = sb("rows", [NROW, P])
        cols = sb("cols", [P, NROW])
        ms = sb("ms", [P, 4 * TT + MT])
        rms = sb("rms", [P, 4 * TT + MT])
        u_pad = sb("u_pad", [P, SEQ + CONVK - 1])
        cxs = sb("cxs", [P, SEQ])
        ytap = sb("ytap", [P, SEQ])
        gex = sb("gex", [P, 2, SEQ])
        neg_half = sb("neg_half", [P, 1])
        iota16 = sb("iota16", [P, TOPK])
        xmax = sb("xmax", [P, TT, XH])
        xneg = sb("xneg", [P, TT, XH])
        xsum = sb("xsum", [P, TT, XH])
        xinv = sb("xinv", [P, TT, XH])
        cur = sb("cur", [P, 2, NK])
        top_v = sb("top_v", [P, 2, TOPK])
        top_i = sb("top_i", [P, 2, TOPK], U32)
        top_f = sb("top_f", [P, 2, TOPK])
        best = sb("best", [P, 2, TOPK])
        pos = sb("pos", [P, TOPK], U32)
        pos_ab = sb("pos_ab", [P, 2, TOPK], U32)
        pos_f = sb("pos_f", [P, 2, TOPK])
        sel = sb("sel", [P, 2, TOPK])
        idx_u = sb("idx_u", [P, 2, TOPK], U32)
        idx_v = sb("idx_v", [P, 2, TOPK], U32)
        neg_best = sb("neg_best", [P, 2])
        gate_e = sb("gate_e", [P, 2, TOPK])
        gate_s = sb("gate_s", [P, 2])
        gate_r = sb("gate_r", [P, 2])
        dots = sb("dots", [P, 2, TOPK])
        gl = sb("gl", [P, 4, TOPK])
        wgt = sb("wgt", [P, 2, TOPK])

        jb = ctx.enter_context(nc.psum_tensor("jb", [P, BANKS, BANK], F32))
        ab = ctx.enter_context(nc.psum_tensor("ab", [P, 4, BANK], F32))

        qT, kT = qk[:, 0:KT, :], qk[:, KT:2 * KT, :]
        yconv, merged = ymix[:, 0:KT, :], ymix[:, KT:2 * KT, :]
        yflat = yconv.rearrange("p k t -> p (k t)")
        mem_tok = yflat[:, 0:MT * D].rearrange("p (i d) -> p i d", i=MT)
        keys_raw = yflat[:, 0:NQ * P].rearrange("p (c n) -> p c n", c=NQ)
        zs, spb, wbuf = (workf[:, 3 * BANK * n:3 * BANK * n + SPAN] for n in range(3))
        xnb = [workf[:, 0:D], workf[:, D:2 * D]]
        memT = workf[:, 2 * D:2 * D + KT * M].rearrange("p (k m) -> p k m", k=KT)
        diag = workf[:, 0:TOPK * P].rearrange("p (e n) -> p e n", e=TOPK)
        xcur = workf[:, 2 * D:3 * D]
        oT = merged
        q3 = workf[:, 3 * D:4 * D].rearrange("p (b t) -> p b t", b=2)
        cand = workf[:, 4 * D:4 * D + TOPK * TOPK]
        hot = workf[:, 4 * D + TOPK * TOPK:4 * D + 2 * TOPK * TOPK].rearrange("p (k s) -> p k s", k=TOPK)
        memf = memkv[:, :, :].rearrange("p a d -> p (a d)")
        memk = memf[:, 0:KT * M].rearrange("p (k m) -> p k m", k=KT)
        memv = memf[:, KT * M:KT * M + MT * D].rearrange("p (i d) -> p i d", i=MT)
        g_ffn = memf[:, 0:D]
        g_fin = wring[:, 0, :, :].rearrange("p k n -> p (k n)")
        probsT = kT.rearrange("p k t -> p (k t)").rearrange("p (b h t) -> p b h t", b=MT, h=XH)
        qkf = qk[:, :, :].rearrange("p a t -> p (a t)")
        scores = qkf.rearrange("p (i c n) -> p i c n", i=TT, c=NQ)
        scores_g = qkf.rearrange("p (g c n) -> p g c n", g=GROUPS, c=2)
        URING, VRING = 8, 4
        u_rows = ymix[:, :, :].rearrange("p a t -> p (a t)").rearrange("p (s d) -> p s d", s=URING)
        v_rows = memkv

        bank_done = [sem(f"bank_done{b}") for b in range(BANKS)]
        bank_free = [sem(f"bank_free{b}") for b in range(BANKS)]
        w_ready = [sem(f"w_ready{s}") for s in range(RING)]
        x_in = [sem(f"x_in{i}") for i in range(TT)]
        par_in, keys_in, mem_in, gffn_in, gfin_in = (
            sem(n) for n in ("par_in", "keys_in", "mem_in", "gffn_in", "gfin_in"))
        consts = sem("consts")
        pads = sem("pads")
        cols_rdy = sem("cols_rdy")
        sq_done = sem("sq_done")
        eps_done = sem("eps_done")
        rms_done = sem("rms_done")
        xn_done = sem("xn_done")
        x3_done = sem("x3_done")
        z_done = sem("z_done")
        zs_done = sem("zs_done")
        zc_done = sem("zc_done")
        ez_done = sem("ez_done")
        ln_done = sem("ln_done")
        sp_done = sem("sp_done")
        spm_done = sem("spm_done")
        c_done = sem("c_done")
        arg_done = sem("arg_done")
        argm_done = sem("argm_done")
        wt_done = sem("wt_done")
        y_done = sem("y_done")
        y_out = sem("y_out")
        cu_done = sem("cu_done")
        gs_done = sem("gs_done")
        ga_done = sem("ga_done")
        xm_done = sem("xm_done")
        xp_done = sem("xp_done")
        h_done = sem("h_done")
        sc_out = sem("sc_out")
        tk = sem("tk")
        best_rdy = sem("best_rdy")
        idx_rdy = sem("idx_rdy")
        idx_cp = sem("idx_cp")
        slot_ok = sem("slot_ok")
        gate_rdy = sem("gate_rdy")
        u_ready = [sem(f"u_ready{s}") for s in range(URING)]
        v_ready = [sem(f"v_ready{s}") for s in range(VRING)]
        u_used = sem("u_used")
        v_free = sem("v_free")
        xc_done = sem("xc_done")
        gl_done = sem("gl_done")
        gle_done = sem("gle_done")
        wgt_rdy = sem("wgt_rdy")
        diag_rdy = sem("diag_rdy")
        acc_free = sem("acc_free")
        hadd = sem("hadd")
        fin_done = sem("fin_done")
        out_done = [sem(f"out_done{b}") for b in range(2)]

        block = ctx.enter_context(nc.Block())

        def wait_free(eng, job):
            if job >= BANKS:
                eng.wait_ge(bank_free[job % BANKS], job // BANKS)

        def wait_job(eng, job):
            eng.wait_ge(bank_done[job % BANKS], job // BANKS + 1)

        def wait_taken(eng, job):
            eng.wait_ge(bank_free[job % BANKS], job // BANKS + 1)

        def wait_all_taken(eng, upto):
            for job in range(upto - BANKS, upto):
                wait_taken(eng, job)

        @block.sync
        def _(sp):
            for i in range(TT):
                sp.dma_start(h[:, i, :], x[0, P * i:P * (i + 1), :]).then_inc(x_in[i], 16)
            for n, blk in enumerate(blocks):
                for s, (w2, c, _) in enumerate(blk):
                    if n:
                        wait_job(sp, blocks[n - 1][s][2])
                    sp.dma_start(wring[:, s, :, :],
                                 w2.rearrange("(k p) n -> p k n", p=P)[:, :, P * c:P * (c + 1)]).then_inc(w_ready[s], 16)
                if n == B_WO:
                    wait_all_taken(sp, J_GA)
                    sp.dma_start(mem_tok, mem[0].rearrange("(i p) d -> p i d", p=P)).then_inc(mem_in, 16)
                if n == B_XO:
                    wait_job(sp, job_s(TT - 1) + 1)
                    sp.dma_start(g_ffn, norm_ffn[0].partition_broadcast(P)).then_inc(gffn_in, 16)
            wait_job(sp, blocks[-1][0][2])
            sp.dma_start(g_fin, norm_final.partition_broadcast(P)).then_inc(gfin_in, 16)
            for i in range(TT):
                sp.wait_ge(fin_done, i + 1)
                sp.dma_start(out[0, P * i:P * (i + 1), :], xnb[i % 2]).then_inc(out_done[i % 2], 16)
            for b in range(2):
                sp.wait_ge(out_done[b], 16 * TT // 2)

        @block.gpsimd
        def _(pool):
            pool.memset(ident[:, :], 0.0).then_inc(consts, 1)
            pool.memset(ones[:, :], 1.0).then_inc(consts, 1)
            pool.memset(nmask[:, :], 0.0).then_inc(consts, 1)
            pool.memset(neg_half[:, :], -0.5).then_inc(consts, 1)
            pool.wait_ge(consts, 4)
            pool.affine_select(out=ident[:, :], in_=ident[:, :], compare_op=ALU.not_equal, fill=1.0, base=0,
                               pattern=[[-1, P]], channel_multiplier=1).then_inc(consts, 1)
            pool.affine_select(out=tri[:, :], in_=ones[:, :], compare_op=ALU.is_ge, fill=0.0, base=0,
                               pattern=[[-1, P]], channel_multiplier=1).then_inc(consts, 1)
            pool.affine_select(out=cmask[:, :], in_=ones[:, :], compare_op=ALU.is_gt, fill=0.0, base=0,
                               pattern=[[1, P]], channel_multiplier=-1).then_inc(consts, 1)
            pool.affine_select(out=nmask[:, :], in_=nmask[:, :], compare_op=ALU.is_gt, fill=-1.0e30, base=0,
                               pattern=[[1, P]], channel_multiplier=-1).then_inc(consts, 1)
            pool.iota(iota16[:, :], pattern=[[1, TOPK]], base=0, channel_multiplier=0,
                      allow_small_or_imprecise_dtypes=True).then_inc(consts, 1)

            def inverse_rms(lo, hi):
                for n in range(lo, hi):
                    pool.wait_ge(sq_done, n + 1)
                    pool.tensor_scalar(rms[:, n:n + 1], ms[:, n:n + 1], EPS, None, ALU.add).then_inc(eps_done, 1)
                    pool.wait_ge(eps_done, n + 1)
                    pool.tensor_tensor(rms[:, n:n + 1], rms[:, n:n + 1], neg_half[:, :],
                                       ALU.pow).then_inc(rms_done, 1)

            def gather(table, index, to, ready):
                pool.indirect_dma_start(out=to, out_offset=None, in_=table,
                                        in_offset=bass.IndirectOffsetOnAxis(ap=index, axis=0)).then_inc(ready, 16)

            inverse_rms(0, 3 * TT + MT)
            pool.wait_ge(idx_rdy, 1)
            pool.sem_inc(v_free, VRING)
            pool.sem_inc(acc_free, 2)
            for e in range(TOPK):
                if e >= URING:
                    pool.wait_ge(u_used, e - URING + 1)
                gather(peer_u[0], idx_u[:, 0, e:e + 1], u_rows[:, e % URING, :], u_ready[e % URING])

            def pair(i, last):
                for b in range(2):
                    with_u = not (last and b == 1)
                    pool.wait_ge(idx_rdy, i * 2 + (b + 1))
                    pool.sem_inc(slot_ok, 1)
                    pool.tensor_copy(idx_v[:, b, :], idx_u[:, b, :]).then_inc(idx_cp, 1)
                    pool.wait_ge(idx_cp, i * 2 + (b + 1))
                    pool.sem_inc(slot_ok, 1)
                    if with_u:
                        pool.wait_ge(idx_rdy, i * 2 + (b + 2))
                        pool.sem_inc(slot_ok, 1)
                    for e in range(TOPK):
                        if with_u:
                            pool.wait_ge(u_used, i * (2 * TOPK) + (TOPK * (b + 1) + e - URING + 1))
                            pool.sem_inc(slot_ok, 1)
                            gather(peer_u[0], idx_u[:, 1 - b, e:e + 1], u_rows[:, e % URING, :], u_ready[e % URING])
                        pool.wait_ge(v_free, i * (2 * TOPK) + (TOPK * b + e + 1))
                        pool.sem_inc(slot_ok, 1)
                        gather(peer_v[0], idx_v[:, b, e:e + 1], v_rows[:, e % VRING, :], v_ready[e % VRING])

            with pool.Fori(0, PAIRS - 1) as i:
                pair(i, False)
            pair(PAIRS - 1, True)
            inverse_rms(3 * TT + MT, 4 * TT + MT)

        @block.tensor
        def _(pe):
            pe.wait_ge(consts, 8)

            def transposes(job, tiles):
                wait_free(pe, job)
                for n, t in enumerate(tiles):
                    mm = pe.transpose(jb[:, job % BANKS, P * n:P * (n + 1)], t, ident[:, :])
                mm.then_inc(bank_done[job % BANKS], 1)

            def norm_transposes(job, done, count, tiles, source):
                for i in range(tiles):
                    pe.wait_ge(done, count + i + 1)
                    for half in range(2):
                        transposes(job + 2 * i + half, [source(i)[:, P * k:P * (k + 1)]
                                                        for k in range(4 * half, 4 * half + 4)])

            def feature_job(job, blk, s, act, n):
                pe.wait_ge(w_ready[s], 16 * (blk + 1))
                wait_free(pe, job)
                for k in range(KT):
                    mm = pe.matmul(jb[:, job % BANKS, 0:n], wring[:, s, k, :], act[:, k, :],
                                   start=(k == 0), stop=(k == KT - 1))
                mm.then_inc(bank_done[job % BANKS], 1)

            def token_jobs(job, blk, act, tiles):
                for half in range(2):
                    for s in range(4 * half, 4 * half + 4):
                        pe.wait_ge(w_ready[s], 16 * (blk + 1))
                    for i in range(tiles):
                        j = job + tiles * half + i
                        wait_free(pe, j)
                        for k in range(KT):
                            mm = pe.matmul(jb[:, j % BANKS, :], act[:, k, P * i:P * (i + 1)],
                                           wring[:, 4 * half:4 * half + 4, k, :],
                                           start=(k == 0), stop=(k == KT - 1))
                        mm.then_inc(bank_done[j % BANKS], 1)

            pe.wait_ge(par_in, 64)
            pe.transpose(jb[:, 0, 0:NROW], rows[:, :], ident[0:NROW, 0:NROW]).then_inc(bank_done[0], 1)
            norm_transposes(J_NORM1, xn_done, 0, TT, lambda i: xnb[i % 2])
            pe.wait_ge(keys_in, 16)
            for n in range(4):
                transposes(J_KEYS + n, [keys_raw[:, 4 * n + c, :] for c in range(4)])

            wait_all_taken(pe, J_KEYS)
            for n in range(2 * KT):
                feature_job(J_QK + n, n // RING, n % RING, xT, SEQ)
            token_jobs(J_V, 2, xT, TT)
            wait_all_taken(pe, J_MIX)

            def ab_cols(j, lo, n):
                o = OFF[j] + lo
                return ab[:, o // BANK, o % BANK:o % BANK + n]

            for m in range(KT):
                for b in range(2):
                    hd, r = 2 * m + b, DH * b
                    j = J_MIX + 4 * m + 2 * b
                    s = 4 * (m % 2) + 2 * b
                    if hd:
                        pe.wait_ge(arg_done, hd)
                    for t in range(TT):
                        mm = pe.matmul(ab_cols(t, 0, WID[t]), kT[r:r + DH, m, P * t:P * (t + 1)],
                                       qT[r:r + DH, m, P * t:SEQ], start=True, stop=True)
                    mm.then_inc(z_done, 1)
                    feature_job(j, B_MIX + m // 2, s, xT, SEQ)
                    pe.wait_ge(spm_done, hd + 1)
                    for t in range(TT):
                        for tt in range(t, TT):
                            mm = pe.matmul(ab_cols(t, P * (tt - t), WID[tt]), (tri if tt == t else ones)[:, :],
                                           spb[:, OFF[tt]:OFF[tt] + WID[tt]], start=(tt == t), stop=(tt == TT - 1))
                    mm.then_inc(c_done, 1)
                    feature_job(j + 1, B_MIX + m // 2, s + 1, xT, SEQ)
                    pe.wait_ge(wt_done, hd + 1)
                    if hd:
                        pe.wait_ge(y_out, hd)
                    for t in range(TT):
                        mm = pe.matmul(ab[r:r + DH, 3, P * t:SEQ], vbuf[:, t, P * m + r:P * m + r + DH],
                                       wbuf[:, OFF[t]:OFF[t] + WID[t]], start=(t == 0), stop=(t == TT - 1))
                    mm.then_inc(y_done, 1)

            wait_all_taken(pe, J_WC)
            for m in range(KT):
                feature_job(J_WC + m, B_WC, m, yconv, SEQ)
            pe.wait_ge(y_out, SBH)
            for m in range(KT):
                for c in range(2):
                    feature_job(J_GA + 2 * m + c, B_GA + m // 4, 2 * (m % 4) + c, (xT, qT)[c], SEQ)
            pe.wait_ge(ga_done, 3 * KT)
            token_jobs(J_WO, B_WO, merged, TT)

            norm_transposes(J_MEMT, xn_done, TT, MT, lambda i: xnb[i % 2])
            wait_all_taken(pe, J_XK)
            for m in range(KT):
                feature_job(J_XK + m, B_XK, m, memT, M)
            token_jobs(J_XV, B_XV, memT, MT)

            norm_transposes(J_NORM2, xn_done, TT + MT, TT, lambda i: xnb[i % 2])
            wait_all_taken(pe, J_XQ)
            for m in range(KT):
                feature_job(J_XQ + m, B_XQ, m, xT, SEQ)
            wait_all_taken(pe, J_SP)

            def cross_scores(i):
                for half in range(2):
                    j = job_s(i) + half
                    wait_free(pe, j)
                    for hh in range(2):
                        for k in range(2):
                            kt = 2 * (2 * half + hh) + k
                            mm = pe.matmul(jb[:, j % BANKS, M * hh:M * (hh + 1)], qT[:, kt, P * i:P * (i + 1)],
                                           memk[:, kt, :], start=(k == 0), stop=(k == 1))
                    mm.then_inc(bank_done[j % BANKS], 1)

            cross_scores(0)
            for i in range(TT):
                if i + 1 < TT:
                    cross_scores(i + 1)
                pe.wait_ge(xp_done, 2 * (i + 1))
                for mb in range(MT):
                    transposes(job_p(i) + mb, [xnb[i % 2][:, M * hx + P * mb:M * hx + P * (mb + 1)]
                                               for hx in range(XH)])
            wait_all_taken(pe, J_O)
            for m in range(KT):
                j = J_O + m
                wait_free(pe, j)
                for mb in range(MT):
                    mm = pe.matmul(jb[:, j % BANKS, :], memv[:, mb, P * m:P * (m + 1)], probsT[:, mb, m // 2, :],
                                   start=(mb == 0), stop=(mb == MT - 1))
                mm.then_inc(bank_done[j % BANKS], 1)
            wait_all_taken(pe, J_XO)
            token_jobs(J_XO, B_XO, oT, TT)

            norm_transposes(J_NORM3, x3_done, 0, TT, lambda i: vbuf[:, i, :])
            wait_all_taken(pe, J_PQ)

            def key_scores(j, q_job, c, tiles):
                wait_free(pe, j)
                wait_taken(pe, q_job)
                for i in range(tiles):
                    mm = pe.matmul(jb[:, j % BANKS, P * i:P * (i + 1)], q3[:, c % 2, P * i:P * (i + 1)],
                                   keysT[:, c, :], start=True, stop=True)
                mm.then_inc(bank_done[j % BANKS], 1)

            for c in range(NQ):
                feature_job(job_f(c), B_PQ + c // RING, c % RING, xT[:, :, 0:P], P)
                if c:
                    key_scores(job_k(c - 1), job_f(c - 1), c - 1, 1)
            key_scores(job_k(NQ - 1), job_f(NQ - 1), NQ - 1, 1)

            def weighted_rows(i, b, chore=None):
                pe.wait_ge(acc_free, i * 2 + (b + 1))
                for e in range(TOPK):
                    pe.wait_ge(diag_rdy, i * (2 * TOPK) + (TOPK * b + e + 1))
                    pe.wait_ge(v_ready[e % VRING], i * (2 * TOPK // VRING * 16)
                               + 16 * (TOPK // VRING * b + e // VRING + 1))
                    for c in range(2):
                        mm = pe.matmul(ab[:, 2 * b + c, :], diag[:, e, :],
                                       v_rows[:, e % VRING, BANK * c:BANK * (c + 1)],
                                       start=(e == 0), stop=(e == TOPK - 1))
                    mm.then_inc(v_free, 1)
                    if chore:
                        chore(e)

            for g in range(PH):
                def rest_chore(e):
                    if g and e < 2:
                        key_scores(job_kr(2 * g - 2 + e), job_fr(2 * g - 2 + e), 2 * g - 2 + e, TT - 1)
                    c, k = 2 * g + e // KT, e % KT
                    j = job_fr(c)
                    if k == 0:
                        pe.wait_ge(w_ready[c % RING], 16 * (B_PQR + c // RING + 1))
                        wait_free(pe, j)
                    mm = pe.matmul(jb[:, j % BANKS, 0:REST], wring[:, c % RING, k, :], xT[:, k, P:SEQ],
                                   start=(k == 0), stop=(k == KT - 1))
                    if k == KT - 1:
                        mm.then_inc(bank_done[j % BANKS], 1)

                weighted_rows(g // 2, g % 2, rest_chore)
            for c in (NQ - 2, NQ - 1):
                key_scores(job_kr(c), job_fr(c), c, TT - 1)
            with pe.Fori(PH // 2, PAIRS) as i:
                for b in range(2):
                    weighted_rows(i, b)

        XSCALE = float(XD) ** -0.5

        def take_probs(act, i):
            for mb in range(MT):
                j = job_p(i) + mb
                wait_job(act, j)
                act.activation(probsT[:, mb, :, P * i:P * (i + 1)],
                               jb[:, j % BANKS, :].rearrange("p (h t) -> p h t", h=XH),
                               ACT.Copy).then_inc(bank_free[j % BANKS], 1)

        def gate_exp(act, g, b):
            act.wait_ge(best_rdy, g + 1)
            act.activation(gate_e[:, b, :], best[:, b, :], ACT.Exp, bias=neg_best[:, b:b + 1],
                           accum_out=gate_s[:, b:b + 1]).then_inc(gate_rdy, 1)

        @block.scalar
        def _(act):
            for n, src in enumerate((norm_mix, norm_xattn, norm_mem)):
                act.dma_start(rows[KT * n:KT * (n + 1), :], src[0].rearrange("(k p) -> k p", p=P)).then_inc(par_in, 16)
            act.dma_start(rows[3 * KT:NROW, :], conv_w[0].rearrange("c (k p) -> (c k) p", p=P)).then_inc(par_in, 16)
            act.dma_start(keys_raw, peer_sub_keys[0].rearrange("h c n d -> n (h c) d")).then_inc(keys_in, 16)

            def mean_square(src, n):
                if n:
                    act.wait_ge(sq_done, n)
                act.activation(ab[:, 2:4, :], src.rearrange("p (c n) -> p c n", c=2), ACT.Square,
                               scale=float(D) ** -0.5, accum_out=ms[:, n:n + 1]).then_inc(sq_done, 1)

            def normed(src, n, slot):
                act.wait_ge(rms_done, n + 1)
                act.activation(xnb[slot], src, ACT.Copy, scale=rms[:, n:n + 1]).then_inc(xn_done, 1)

            for i in range(TT):
                act.wait_ge(x_in[i], 16)
                mean_square(h[:, i, :], i)
                if i >= 2:
                    wait_job(act, J_NORM1 + 2 * (i - 2) + 1)
                normed(h[:, i, :], i, i % 2)

            def take(job, to, n=BANK, **kw):
                wait_job(act, job)
                act.activation(to, jb[:, job % BANKS, 0:n], kw.get("func", ACT.Copy),
                               scale=kw.get("scale", 1.0)).then_inc(bank_free[job % BANKS], 1)

            for n in range(2 * KT):
                take(J_QK + n, qk[:, n, :])
            for half in range(2):
                for i in range(TT):
                    take(J_V + TT * half + i, vbuf[:, i, BANK * half:BANK * (half + 1)])

            for m in range(KT):
                for b in range(2):
                    hd, r = 2 * m + b, DH * b
                    act.wait_ge(zc_done, hd + 1)
                    act.activation(spb, spb, ACT.Exp).then_inc(ez_done, 1)
                    act.wait_ge(ez_done, hd + 1)
                    act.activation(spb, spb, ACT.Ln, bias=1.0).then_inc(ln_done, 1)
                    if b == 0:
                        if m:
                            wait_taken(act, J_MIX + 4 * (m - 1) + 1)
                        take(J_MIX + 4 * m, cxs[:, :])
                    act.wait_ge(argm_done, hd + 1)
                    act.activation(wbuf, zs, ACT.Exp).then_inc(wt_done, 1)
                    if b == 1:
                        take(J_MIX + 4 * m + 3, merged[:, m, :], func=ACT.Exp, scale=-1.0)
                    act.wait_ge(y_done, hd + 1)
                    act.activation(qT[r:r + DH, m, :], ab[r:r + DH, 3, :], ACT.Copy).then_inc(y_out, 1)

            for m in range(KT):
                if m >= 2:
                    act.wait_ge(ga_done, 3 * (m - 1))
                take(J_GA + 2 * m, gex[:, m % 2, :], func=ACT.Exp, scale=-1.0)

            act.wait_ge(mem_in, 16)
            for i in range(MT):
                mean_square(mem_tok[:, i, :], TT + i)
                normed(mem_tok[:, i, :], TT + i, i % 2)
            for m in range(KT):
                take(J_XK + m, memk[:, m, :], n=M)
            for half in range(2):
                for i in range(MT):
                    take(J_XV + MT * half + i, memv[:, i, BANK * half:BANK * (half + 1)])

            wait_all_taken(act, J_MEMT)
            for i in range(TT):
                mean_square(h[:, i, :], TT + MT + i)
                if i >= 2:
                    wait_job(act, J_NORM2 + 2 * (i - 2) + 1)
                else:
                    wait_job(act, J_MEMT + 2 * MT - 1)
                normed(h[:, i, :], TT + MT + i, i % 2)
            for m in range(KT):
                take(J_XQ + m, qT[:, m, :])
            for i in range(TT):
                act.wait_ge(xm_done, 2 * (i + 1))
                wait_job(act, job_p(i - 2) + 1 if i >= 2 else J_XQ - 1)
                for hx in range(XH):
                    j = job_s(i) + hx // 2
                    ex = act.activation(xnb[i % 2][:, M * hx:M * (hx + 1)],
                                        jb[:, j % BANKS, M * (hx % 2):M * (hx % 2 + 1)], ACT.Exp,
                                        scale=XSCALE, bias=xneg[:, i, hx:hx + 1], accum_out=xsum[:, i, hx:hx + 1])
                    if hx % 2:
                        ex.then_inc(bank_free[j % BANKS], 1)
                if i:
                    take_probs(act, i - 1)
            take_probs(act, TT - 1)
            for m in range(KT):
                take(J_O + m, oT[:, m, :])

            for i in range(TT):
                wait_taken(act, J_XO + TT + i)
                mean_square(h[:, i, :], 2 * TT + MT + i)

            def take_key_scores(j, c, lo, hi, scored):
                wait_job(act, j)
                act.activation(scores[:, lo:hi, c, :],
                               jb[:, j % BANKS, 0:P * (hi - lo)].rearrange("p (i n) -> p i n", i=hi - lo),
                               ACT.Copy).then_inc(bank_free[j % BANKS], 1)
                wait_taken(act, j)
                act.sem_inc(sc_out, scored)

            for c in range(NQ):
                if c >= 2:
                    wait_job(act, job_k(c - 2))
                take(job_f(c), q3[:, c % 2, 0:P], n=P)
                if c:
                    take_key_scores(job_k(c - 1), c - 1, 0, 1, 1)
                if c in (6, 10):
                    gate_exp(act, (c - 6) // 4, (c - 6) // 4)
            take_key_scores(job_k(NQ - 1), NQ - 1, 0, 1, 1)

            def take_rest_scores(g):
                for c in (2 * g, 2 * g + 1):
                    take_key_scores(job_kr(c), c, 1, TT, 1 if c < NQ - 1 else 2 * GROUPS - 2 * NQ + 1)

            def take_rest_queries(g):
                for c in (2 * g, 2 * g + 1):
                    wait_job(act, job_kr(c - 2) if g else job_k(NQ - 2 + c))
                    take(job_fr(c), q3[:, c % 2, 0:REST], n=REST)

            def pair(i, first, last):
                for b in range(2):
                    act.wait_ge(gl_done, i * 16 + (8 * b + 4))
                    act.activation(gl[:, 2, :], gl[:, 1, :], ACT.Exp, scale=-GELU_C).then_inc(gle_done, 1)
                    act.wait_ge(wgt_rdy, i * 2 + (b + 1))
                    for e in range(TOPK):
                        if not (first and b == 0):
                            act.wait_ge(v_free, i * (2 * TOPK) + (TOPK * (b - 1) + e + 1 + VRING))
                        act.activation(diag[:, e, :], ident[:, :], ACT.Copy,
                                       scale=wgt[:, b, e:e + 1]).then_inc(diag_rdy, 1)
                    if isinstance(i, int) and i < PH // 2:
                        if 2 * i + b:
                            take_rest_scores(2 * i + b - 1)
                        take_rest_queries(2 * i + b)
                    if not last:
                        gate_exp(act, i * 2 + (b + 2), b)

            for i in range(PH // 2):
                pair(i, i == 0, False)
            take_rest_scores(PH - 1)
            with act.Fori(PH // 2, PAIRS - 1) as i:
                pair(i, False, False)
            pair(PAIRS - 1, False, True)

            for i in range(TT):
                act.wait_ge(hadd, 1)
                mean_square(h[:, i, :], 3 * TT + MT + i)

        @block.vector
        def _(dve):
            dve.memset(u_pad[:, :], 0.0).then_inc(pads, 1)

            wait_job(dve, J_PARAM)
            dve.tensor_copy(cols[:, :], jb[:, 0, 0:NROW]).then_inc(bank_free[0], 1)
            wait_taken(dve, J_PARAM)

            def take_normed(job, i, to, g0):
                for half in range(2):
                    j = job + 2 * i + half
                    wait_job(dve, j)
                    src = jb[:, j % BANKS, :].rearrange("p (k t) -> p k t", k=4)
                    dst = to[:, 4 * half:4 * half + 4, P * i:P * (i + 1)]
                    if g0 is None:
                        dve.tensor_copy(dst, src).then_inc(bank_free[j % BANKS], 1)
                    else:
                        gain = cols[:, g0 + 4 * half:g0 + 4 * half + 4].unsqueeze(2).to_broadcast([P, 4, P])
                        dve.tensor_tensor(dst, src, gain, ALU.mult).then_inc(bank_free[j % BANKS], 1)

            for i in range(TT + 1):
                if i:
                    take_normed(J_NORM1, i - 1, xT, 0)
            for n in range(4):
                j = J_KEYS + n
                wait_job(dve, j)
                dve.tensor_copy(keysT[:, 4 * n:4 * n + 4, :],
                                jb[:, j % BANKS, :].rearrange("p (c n) -> p c n", c=4)).then_inc(bank_free[j % BANKS], 1)
            dve.memset(zs[:, OFF[1] + WID[1]:OFF[2]], 0.0).then_inc(pads, 1)
            dve.memset(spb[:, OFF[1] + WID[1]:OFF[2]], 0.0).then_inc(pads, 1)
            dve.wait_ge(pads, 3)

            def blocks_of(t):
                return [t[:, 0:BANK], t[:, BANK:BANK + 3 * P].unsqueeze(1)]

            z_parts = [(ab[:, 0, :], lambda t: t[:, 0:BANK]),
                       (ab[:, 1, 0:WID[1]], lambda t: t[:, OFF[1]:OFF[1] + WID[1]]),
                       (ab[:, 2, 0:WID[1]], lambda t: t[:, OFF[2]:OFF[2] + WID[1]])]

            def diagonal(t, op, mask, done):
                for n in range(TT):
                    d = t[:, OFF[n]:OFF[n] + P]
                    last = dve.tensor_tensor(d, d, mask[:, :], op)
                last.then_inc(done, 1)

            def sigmoid_tail(m):
                wait_taken(dve, J_MIX + 4 * m + 3)
                dve.tensor_scalar(merged[:, m, :], merged[:, m, :], 1.0, None, ALU.add).then_inc(gs_done, 1)
                dve.wait_ge(gs_done, 2 * m + 1)
                dve.reciprocal(merged[:, m, :], merged[:, m, :]).then_inc(gs_done, 1)

            for m in range(KT):
                for b in range(2):
                    hd = 2 * m + b
                    dve.wait_ge(z_done, hd + 1)
                    if hd:
                        dve.wait_ge(wt_done, hd)
                    for ps, part in z_parts:
                        last = dve.tensor_scalar(part(zs), ps, float(DH) ** -0.5, None, ALU.mult)
                    last.then_inc(zs_done, 1)
                    dve.wait_ge(zs_done, hd + 1)
                    dve.tensor_scalar(spb, zs, SP_CAP, None, ALU.min).then_inc(zc_done, 1)
                    dve.wait_ge(ln_done, hd + 1)
                    dve.tensor_tensor(spb, spb, zs, ALU.max).then_inc(sp_done, 1)
                    dve.wait_ge(sp_done, hd + 1)
                    diagonal(spb, ALU.mult, cmask, spm_done)
                    j = J_MIX + 4 * m + 2
                    if b == 1:
                        wait_job(dve, j)
                        dve.wait_ge(cu_done, 3 * (m + 1))
                        dve.tensor_tensor(yconv[:, m, :], jb[:, j % BANKS, :], ytap[:, :],
                                          ALU.mult).then_inc(bank_free[j % BANKS], 1)
                    dve.wait_ge(c_done, hd + 1)
                    for ps, part in z_parts:
                        last = dve.tensor_tensor(part(zs), part(zs), ps, ALU.subtract)
                    last.then_inc(arg_done, 1)
                    dve.wait_ge(arg_done, hd + 1)
                    diagonal(zs, ALU.min, nmask, argm_done)
                    if b == 0:
                        if m:
                            sigmoid_tail(m - 1)
                        j = J_MIX + 4 * m + 1
                        wait_job(dve, j)
                        wait_taken(dve, j - 1)
                        dve.tensor_tensor(u_pad[:, CONVK - 1:], jb[:, j % BANKS, :], cxs[:, :],
                                          ALU.mult).then_inc(bank_free[j % BANKS], 1)
                        wait_taken(dve, j)
                        for c in range(CONVK):
                            tap = cols[:, KT * (3 + c) + m:KT * (3 + c) + m + 1]
                            if c == 0:
                                if m:
                                    wait_taken(dve, J_MIX + 4 * (m - 1) + 2)
                                st = dve.tensor_scalar(ytap[:, :], u_pad[:, 0:SEQ], tap, None, ALU.mult)
                            else:
                                dve.wait_ge(cu_done, 3 * m + c)
                                st = dve.scalar_tensor_tensor(out=ytap[:, :], in0=u_pad[:, c:c + SEQ], scalar=tap,
                                                              in1=ytap[:, :], op0=ALU.mult, op1=ALU.add)
                            st.then_inc(cu_done, 1)
            sigmoid_tail(KT - 1)

            for m in range(KT):
                j = J_WC + m
                wait_job(dve, j)
                dve.wait_ge(gs_done, 2 * (m + 1))
                dve.tensor_tensor(merged[:, m, :], jb[:, j % BANKS, :], merged[:, m, :],
                                  ALU.mult).then_inc(bank_free[j % BANKS], 1)
            for m in range(KT):
                j = J_GA + 2 * m
                gx = gex[:, m % 2, :]
                wait_taken(dve, j)
                dve.tensor_scalar(gx, gx, 1.0, None, ALU.add).then_inc(ga_done, 1)
                dve.wait_ge(ga_done, 3 * m + 1)
                dve.reciprocal(gx, gx).then_inc(ga_done, 1)
                dve.wait_ge(ga_done, 3 * m + 2)
                wait_job(dve, j + 1)
                dve.tensor_tensor(gx, jb[:, (j + 1) % BANKS, :], gx, ALU.mult).then_inc(bank_free[(j + 1) % BANKS], 1)
                wait_taken(dve, j + 1)
                wait_taken(dve, J_WC + m)
                dve.tensor_tensor(merged[:, m, :], merged[:, m, :], gx, ALU.add).then_inc(ga_done, 1)

            def residual(job):
                for half in range(2):
                    for i in range(TT):
                        j = job + TT * half + i
                        wait_job(dve, j)
                        hh = h[:, i, BANK * half:BANK * (half + 1)]
                        dve.tensor_tensor(hh, jb[:, j % BANKS, :], hh, ALU.add).then_inc(bank_free[j % BANKS], 1)

            residual(J_WO)
            for i in range(MT + 1):
                if i:
                    take_normed(J_MEMT, i - 1, memT, 2 * KT)
            for i in range(TT + 1):
                if i:
                    take_normed(J_NORM2, i - 1, xT, KT)

            for i in range(TT):
                for half in range(2):
                    j = job_s(i) + half
                    wait_job(dve, j)
                    rd = dve.tensor_reduce(xmax[:, i, 2 * half:2 * half + 2],
                                           jb[:, j % BANKS, :].rearrange("p (h m) -> p h m", h=2), AX.X, ALU.max)
                rd.then_inc(xm_done, 1)
                dve.wait_ge(xm_done, 2 * i + 1)
                dve.tensor_scalar(xneg[:, i, :], xmax[:, i, :], -XSCALE, None, ALU.mult).then_inc(xm_done, 1)
                for half in range(2):
                    wait_taken(dve, job_s(i) + half)
                dve.reciprocal(xinv[:, i, :], xsum[:, i, :]).then_inc(xp_done, 1)
                dve.wait_ge(xp_done, 2 * i + 1)
                pr = xnb[i % 2].rearrange("p (h m) -> p h m", h=XH)
                dve.tensor_tensor(pr, pr, xinv[:, i, :].unsqueeze(2).to_broadcast([P, XH, M]),
                                  ALU.mult).then_inc(xp_done, 1)

            residual(J_XO)
            dve.wait_ge(gffn_in, 16)
            for i in range(TT + 1):
                n = 2 * TT + MT + i
                if i < TT:
                    dve.wait_ge(rms_done, n + 1)
                    dve.scalar_tensor_tensor(out=vbuf[:, i, :], in0=h[:, i, :], scalar=rms[:, n:n + 1], in1=g_ffn,
                                             op0=ALU.mult, op1=ALU.mult).then_inc(x3_done, 1)
                if i:
                    take_normed(J_NORM3, i - 1, xT, None)

            def select(g, b):
                n = [0]

                def after(ins):
                    ins.then_inc(tk, 1)
                    n[0] += 1
                    dve.wait_ge(tk, n[0])

                def top16(vals, src, where):
                    after(dve.max(vals[:, 0:8], src))
                    after(dve.max_index(where[:, 0:8], vals[:, 0:8], src))
                    after(dve.match_replace(src, vals[:, 0:8], src, LOWEST))
                    after(dve.max(vals[:, 8:16], src))
                    after(dve.max_index(where[:, 8:16], vals[:, 8:16], src))

                dve.wait_ge(sc_out, g * 2 + 2)
                after(dve.tensor_copy(cur[:, :, :], scores_g[:, g, :, :] if isinstance(g, int)
                                      else scores_g[:, bass.ds(g, 1), :, :].rearrange("p g c n -> p (g c) n")))
                for c in range(2):
                    top16(top_v[:, c, :], cur[:, c, :], top_i[:, c, :])
                candv = cand.rearrange("p (a b) -> p a b", a=TOPK)
                after(dve.tensor_tensor(candv, top_v[:, 0, :].unsqueeze(2).to_broadcast([P, TOPK, TOPK]),
                                        top_v[:, 1, :].unsqueeze(1).to_broadcast([P, TOPK, TOPK]), ALU.add))
                after(dve.tensor_scalar(top_f[:, 0, :], top_i[:, 0, :], float(NK), None, ALU.mult))
                after(dve.tensor_copy(top_f[:, 1, :], top_i[:, 1, :]))
                top16(best[:, b, :], cand, pos[:, :])
                dve.tensor_scalar(neg_best[:, b:b + 1], best[:, b, 0:1], -1.0, None, ALU.mult).then_inc(best_rdy, 1)
                after(dve.tensor_scalar(pos_ab[:, 0, :], pos[:, :], 4, None, ALU.logical_shift_right))
                after(dve.tensor_scalar(pos_ab[:, 1, :], pos[:, :], TOPK - 1, None, ALU.bitwise_and))
                after(dve.tensor_copy(pos_f[:, :, :], pos_ab[:, :, :]))
                for c in range(2):
                    after(dve.tensor_tensor(hot, pos_f[:, c, :].unsqueeze(2).to_broadcast([P, TOPK, TOPK]),
                                            iota16[:, :].unsqueeze(1).to_broadcast([P, TOPK, TOPK]), ALU.is_equal))
                    after(dve.tensor_tensor(hot, hot, top_f[:, c, :].unsqueeze(1).to_broadcast([P, TOPK, TOPK]),
                                            ALU.mult))
                    after(dve.tensor_reduce(sel[:, c, :], hot, AX.X, ALU.add))
                dve.sem_clear(tk)
                dve.tensor_tensor(idx_u[:, b, :], sel[:, 0, :], sel[:, 1, :], ALU.add).then_inc(idx_rdy, 1)

            dve.wait_ge(consts, 9)
            select(0, 0)
            select(1, 1)

            def tile_of(t, q):
                return t[:, q, :] if isinstance(q, int) else t[:, bass.ds(q, 1), :].rearrange("p a d -> p (a d)")

            def add_experts(i, b):
                dve.wait_ge(v_free, i * (2 * TOPK) + (TOPK * (b + 1) + VRING))
                hh = tile_of(h, i // (PH // 2))
                return dve.tensor_tensor(hh, ab[:, 2 * b:2 * b + 2, :].rearrange("p c n -> p (c n)"), hh, ALU.add)

            def pair(i, first, last):
                for b in range(2):
                    if b == 0:
                        dve.tensor_copy(xcur, tile_of(vbuf, i // (PH // 2))).then_inc(xc_done, 1)
                        dve.wait_ge(xc_done, i + 1)
                    for e in range(TOPK):
                        dve.wait_ge(u_ready[e % URING], i * (2 * TOPK // URING * 16)
                                    + 16 * (TOPK // URING * b + e // URING + 1))
                        u = u_rows[:, e % URING, :]
                        dve.tensor_tensor_reduce(out=u, in0=u, in1=xcur, scale=1.0, scalar=0.0, op0=ALU.mult,
                                                 op1=ALU.add, accum_out=dots[:, b, e:e + 1]).then_inc(u_used, 1)
                    a = dots[:, b, :]
                    n = [0]

                    def step(ins):
                        ins.then_inc(gl_done, 1)
                        n[0] += 1

                    def wait_steps():
                        dve.wait_ge(gl_done, i * 16 + (8 * b + n[0]))

                    dve.wait_ge(u_used, i * (2 * TOPK) + TOPK * (b + 1))
                    step(dve.tensor_tensor(gl[:, 0, :], a, a, ALU.mult))
                    wait_steps()
                    step(dve.tensor_scalar(gl[:, 0, :], gl[:, 0, :], 0.044715, 1.0, ALU.mult, ALU.add))
                    wait_steps()
                    step(dve.tensor_tensor(gl[:, 1, :], gl[:, 0, :], a, ALU.mult))
                    wait_steps()
                    step(dve.tensor_scalar(gl[:, 1, :], gl[:, 1, :], GELU_FLOOR, None, ALU.max))
                    dve.wait_ge(gate_rdy, i * 2 + (b + 1))
                    step(dve.tensor_tensor(gl[:, 3, :], a, gate_e[:, b, :], ALU.mult))
                    step(dve.reciprocal(gate_r[:, b:b + 1], gate_s[:, b:b + 1]))
                    dve.wait_ge(gle_done, i * 2 + (b + 1))
                    step(dve.tensor_scalar(gl[:, 2, :], gl[:, 2, :], 1.0, None, ALU.add))
                    wait_steps()
                    step(dve.reciprocal(gl[:, 2, :], gl[:, 2, :]))
                    wait_steps()
                    if not first:
                        dve.wait_ge(diag_rdy, i * (2 * TOPK) + TOPK * (b - 1))
                    dve.scalar_tensor_tensor(out=wgt[:, b, :], in0=gl[:, 3, :], scalar=gate_r[:, b:b + 1],
                                             in1=gl[:, 2, :], op0=ALU.mult, op1=ALU.mult).then_inc(wgt_rdy, 1)
                    if not last:
                        dve.wait_ge(idx_cp, i * 2 + (b + 1))
                        select(i * 2 + (b + 2), b)
                    if not (first and b == 0):
                        add_experts(i - (1 - b), 1 - b).then_inc(acc_free, 1)

            pair(0, True, False)
            with dve.Fori(1, PAIRS - 1) as i:
                pair(i, False, False)
            pair(PAIRS - 1, False, True)
            dve.wait_ge(acc_free, 2 * PAIRS + 1)
            add_experts(PAIRS - 1, 1).then_inc(hadd, 1)

            dve.wait_ge(gfin_in, 16)
            for i in range(TT):
                n = 3 * TT + MT + i
                dve.wait_ge(rms_done, n + 1)
                if i >= 2:
                    dve.wait_ge(out_done[i % 2], 16 * (i // 2))
                dve.scalar_tensor_tensor(out=xnb[i % 2], in0=h[:, i, :], scalar=rms[:, n:n + 1], in1=g_fin,
                                         op0=ALU.mult, op1=ALU.mult).then_inc(fin_done, 1)


_INS = ["x", "mem", "norm_mix", "w_in", "conv_w", "w_branch_attn", "w_branch_conv", "w_out", "norm_xattn", "norm_mem",
        "xattn_wq", "xattn_wk", "xattn_wv", "xattn_wo", "norm_ffn", "peer_w_query", "peer_sub_keys", "peer_u",
        "peer_v", "norm_final"]


def kernel(**inputs):
    import numpy as _np
    import concourse.bacc as _bacc
    from concourse import mybir as _mybir
    from concourse.bass_utils import run_bass_kernel_spmd as _run

    nc = _bacc.Bacc("TRN2", target_bir_lowering=False, num_devices=1)
    arrays, args = {}, []
    for name in _INS:
        a = _np.ascontiguousarray(inputs[name])
        arrays[f"in_{name}_dram"] = a
        args.append(nc.dram_tensor(f"in_{name}_dram", a.shape, _mybir.dt.from_np(a.dtype), kind="ExternalInput").ap())
    shape = inputs["x"].shape
    args.append(nc.dram_tensor("out_0_dram", shape, _mybir.dt.float32, kind="ExternalOutput").ap())
    build_trunk(nc, *args)
    r = _run(nc, [arrays], core_ids=[0])
    return r.results[0]["out_0_dram"]
```

```python
from contextlib import ExitStack

import concourse.bass as bass
from concourse import mybir

F32 = mybir.dt.float32
U32 = mybir.dt.uint32
F32R = mybir.dt.float32r
ALU = mybir.AluOpType
ACT = mybir.ActivationFunctionType
AX = mybir.AxisListType

P = 128
BANK = 512
BANKS = 4
RING = 8
EPS = 1e-6
SP_CAP = 40.0
GELU_C = 2.0 * 0.7978845608028654
GELU_FLOOR = -50.0
LOWEST = -3.0e38


def build_trunk(nc, x, mem, norm_mix, w_in, conv_w, w_branch_attn, w_branch_conv, w_out,
                norm_xattn, norm_mem, xattn_wq, xattn_wk, xattn_wv, xattn_wo,
                norm_ffn, peer_w_query, peer_sub_keys, peer_u, peer_v, norm_final, out):
    D = x.shape[2]
    SEQ = x.shape[1]
    M = mem.shape[1]
    KT = D // P
    TT = SEQ // P
    MT = M // P
    SBH, DH = 16, 64
    XH, XD = 4, D // 4
    PH, NK, TOPK = peer_sub_keys.shape[1], peer_sub_keys.shape[3], 16
    CONVK = conv_w.shape[1]
    NROW = 3 * KT + CONVK * KT
    GROUPS = TT * PH
    PAIRS = GROUPS // 2
    assert SBH * DH == D and (KT, TT, MT, NK, TOPK, PH) == (8, 4, 2, 128, 16, 8)

    WID = [SEQ - P * j for j in range(TT)]
    OFF = [0, BANK, 2 * BANK, 2 * BANK + WID[2]]
    SPAN = OFF[3] + WID[3]

    COLQ, COLK, COLV, COLX, COLB, COLC, COLGA, COLGC = (KT * n for n in range(8))

    J_PARAM = 0
    J_NORM1 = J_PARAM + 1
    J_KEYS = J_NORM1 + 2 * TT
    J_QK = J_KEYS + 4
    J_V = J_QK + 2 * KT
    J_MIX = J_V + 2 * TT
    J_WC = J_MIX + 4 * KT
    J_GA = J_WC + KT
    J_WO = J_GA + 2 * KT
    J_MEMT = J_WO + 2 * TT
    J_XK = J_MEMT + 2 * MT
    J_XV = J_XK + KT
    J_NORM2 = J_XV + 2 * MT
    J_XQ = J_NORM2 + 2 * TT
    J_S = J_XQ + KT
    J_O = J_S + 4
    J_XO = J_O + KT
    J_NORM3 = J_XO + 2
    J_PQ = J_NORM3 + 2
    REST = SEQ - P
    NQ = 2 * PH
    J_SR = J_PQ + 2 * NQ
    J_OR = J_SR + 4 * (TT - 1)
    J_XOR = J_OR + KT
    J_NORM3R = J_XOR + 2 * (TT - 1)
    J_PQR = J_NORM3R + 2 * (TT - 1)
    G_S, G_O, G_N, G_PQ = 0, 1, 3, 4
    G_END = G_PQ + PH

    def job_s(i):
        return J_S if i == 0 else J_SR + 4 * (i - 1)

    def job_p(i):
        return job_s(i) + 2

    def job_f(c):
        return J_PQ + (2 * c - 1 if c else 0)

    def job_k(c):
        return J_PQ + (2 * c + 2 if c < NQ - 1 else 2 * NQ - 1)

    def job_fr(c):
        return J_PQR + 2 * (c - c % 2) + c % 2

    def job_kr(c):
        return job_fr(c) + 2

    def plain(w2, col, job):
        return [(w2, col + s, job + s) for s in range(RING)]

    def by_tokens(w2, col, job, tiles):
        return [(w2, col + s, job + tiles * (s // 4) + tiles - 1) for s in range(RING)]

    w_in2, wa2 = w_in[0], w_branch_attn[0]
    blocks = [plain(w_in2, COLQ, J_QK), plain(w_in2, COLK, J_QK + KT), by_tokens(w_in2, COLV, J_V, TT)]
    B_MIX = len(blocks)
    for m in range(0, KT, 2):
        blocks.append([(w_in2, (COLX, COLC, COLB, COLGC)[s % 4] + m + s // 4, J_MIX + 4 * m + s) for s in range(RING)])
    B_WC = len(blocks)
    blocks.append(plain(w_branch_conv[0], 0, J_WC))
    B_GA = len(blocks)
    for m in range(0, KT, 4):
        blocks.append([((w_in2, COLGA) if s % 2 == 0 else (wa2, 0)) for s in range(RING)])
        blocks[-1] = [(w2, c0 + m + s // 2, J_GA + 2 * m + s) for s, (w2, c0) in enumerate(blocks[-1])]
    B_WO = len(blocks)
    blocks.append(by_tokens(w_out[0], 0, J_WO, TT))
    B_XK = len(blocks)
    blocks.append(plain(xattn_wk[0], 0, J_XK))
    B_XV = len(blocks)
    blocks.append(by_tokens(xattn_wv[0], 0, J_XV, MT))
    B_XQ = len(blocks)
    blocks.append(plain(xattn_wq[0], 0, J_XQ))
    B_XO = len(blocks)
    blocks.append(by_tokens(xattn_wo[0], 0, J_XO, 1))
    B_PQ = len(blocks)
    for c in range(0, NQ, RING):
        blocks.append([(peer_w_query[0], c + s, job_f(c + s)) for s in range(RING)])
    HALF = RING // 2
    B_XOR = len(blocks)
    for half in range(2):
        blocks.append([None] * HALF + [(xattn_wo[0], 4 * half + s, J_XOR + (TT - 1) * half + TT - 2)
                                       for s in range(HALF)])
    B_PQR = len(blocks)
    for c in range(0, NQ, HALF):
        blocks.append([None] * HALF + [(peer_w_query[0], c + s, job_fr(c + s)) for s in range(HALF)])

    with ExitStack() as ctx:
        def sb(name, shape, dt=F32):
            return ctx.enter_context(nc.sbuf_tensor(name, shape, dt))

        def sem(name):
            return ctx.enter_context(nc.semaphore(name))

        def sb_both(name, shape):
            with nc.sbuf_tensor(name + "_r", shape, F32R) as rounded:
                pass
            return sb(name, shape), rounded

        xT, xT_r = sb_both("xT", [P, KT, SEQ])
        qk, qk_r = sb_both("qk", [P, 2 * KT, SEQ])
        vbuf, vbuf_r = sb_both("vbuf", [P, TT, D])
        h = sb("h", [P, TT, D])
        ymix, ymix_r = sb_both("ymix", [P, 2 * KT, SEQ])
        wring = sb("wring", [P, RING, KT, P])
        memkv, memkv_r = sb_both("memkv", [P, 4, D])
        keysT = sb("keysT", [P, NQ, NK])
        workf = sb("workf", [P, 9 * BANK])
        ident = sb("ident", [P, P])
        tri = sb("tri", [P, P], F32R)
        ones_r = sb("ones_r", [P, P], F32R)
        sp_hi = sb("sp_hi", [P, SPAN], F32R)
        sp_lo = sb("sp_lo", [P, SPAN], F32R)
        cmask = sb("cmask", [P, P])
        nmask = sb("nmask", [P, P])
        rows = sb("rows", [NROW, P])
        cols = sb("cols", [P, NROW])
        ms = sb("ms", [P, 4 * TT + MT])
        rms = sb("rms", [P, 4 * TT + MT])
        u_pad = sb("u_pad", [P, SEQ + CONVK - 1])
        cxs = sb("cxs", [P, SEQ])
        ytap = sb("ytap", [P, SEQ])
        neg_half = sb("neg_half", [P, 1])
        iota16 = sb("iota16", [P, TOPK])
        xmax = sb("xmax", [P, TT, XH])
        xneg = sb("xneg", [P, TT, XH])
        xsum = sb("xsum", [P, TT, XH])
        xinv = sb("xinv", [P, TT, XH])
        top_i = sb("top_i", [P, 2, TOPK], U32)
        best = sb("best", [P, 2, TOPK])
        pos = sb("pos", [P, TOPK], U32)
        pos_ab = sb("pos_ab", [P, 2, TOPK], U32)
        idx_u = sb("idx_u", [P, 2, TOPK], U32)
        idx_v = sb("idx_v", [P, 2, TOPK], U32)
        neg_best = sb("neg_best", [P, 2])
        gate_s = sb("gate_s", [P, 2])
        gate_r = sb("gate_r", [P, 2])

        jb = ctx.enter_context(nc.psum_tensor("jb", [P, BANKS, BANK], F32))
        ab = ctx.enter_context(nc.psum_tensor("ab", [P, 4, BANK], F32))

        qT, kT = qk[:, 0:KT, :], qk[:, KT:2 * KT, :]
        yconv, merged = ymix[:, 0:KT, :], ymix[:, KT:2 * KT, :]
        yflat = yconv.rearrange("p k t -> p (k t)")
        mem_tok = yflat[:, 0:MT * D].rearrange("p (i d) -> p i d", i=MT)
        keys_raw = vbuf[:, 0:2, :].rearrange("p a (c n) -> p (a c) n", n=P)
        xq_hi, xq_lo = ymix_r[:, 0:KT, :], ymix_r[:, KT:2 * KT, :]
        yc_hi, yc_lo = memkv_r[:, :, :].rearrange("p a (b t) -> p (a b) t", b=2), ymix_r[:, 0:KT, :]
        xg_hi, xg_lo = vbuf_r[:, :, :].rearrange("p a (b t) -> p (a b) t", b=2), xT_r
        ya_hi, ya_lo = qk_r[:, KT:2 * KT, :], qk_r[:, 0:KT, :]
        xc_hi, xc_lo = ymix_r[:, 0:KT, :], xT_r
        w_hi = sp_hi[:, 0:2 * BANK].rearrange("p (c k n) -> p c k n", c=2, k=KT // 2)
        w_lo = sp_lo[:, 0:2 * BANK].rearrange("p (c k n) -> p c k n", c=2, k=KT // 2)
        zs, spb, wbuf = (workf[:, 3 * BANK * n:3 * BANK * n + SPAN] for n in range(3))
        gex = workf[:, 6 * BANK:8 * BANK].rearrange("p (b t) -> p b t", b=2)
        ones = workf[:, 0:P]
        cur = cxs[:, 0:2 * NK].rearrange("p (c n) -> p c n", c=2)
        top_v, top_f, pos_f, sel, dots, wgt, gate_e = (
            ytap[:, 2 * TOPK * n:2 * TOPK * (n + 1)].rearrange("p (c k) -> p c k", c=2) for n in range(7))
        gl = ytap[:, 14 * TOPK:18 * TOPK].rearrange("p (c k) -> p c k", c=4)
        xnb = [workf[:, 0:D], workf[:, D:2 * D]]
        memT = workf[:, 2 * D:2 * D + KT * M].rearrange("p (k m) -> p k m", k=KT)
        diag = workf[:, 0:TOPK * P].rearrange("p (e n) -> p e n", e=TOPK)
        xcur = workf[:, 2 * D:3 * D]
        oT = qT
        q3 = workf[:, 3 * D:4 * D].rearrange("p (b t) -> p b t", b=2)
        cand = workf[:, 4 * D:4 * D + TOPK * TOPK]
        hot = workf[:, 4 * D + TOPK * TOPK:4 * D + 2 * TOPK * TOPK].rearrange("p (k s) -> p k s", k=TOPK)
        memf = memkv[:, :, :].rearrange("p a d -> p (a d)")
        memk = memf[:, 0:KT * M].rearrange("p (k m) -> p k m", k=KT)
        memv = memf[:, KT * M:KT * M + MT * D].rearrange("p (i d) -> p i d", i=MT)
        g_ffn = vbuf[:, TT - 1, :]
        g_fin = keysT[:, 0:KT, :].rearrange("p c n -> p (c n)")
        probs0T = kT[:, 0:2, :].rearrange("p k t -> p (k t)").rearrange("p (b h t) -> p b h t", b=MT, h=XH)
        probsRT = xT[:, :, P:SEQ].rearrange("p (b h) t -> p b h t", b=MT)
        probs_tok = workf[:, 3 * D:4 * D]
        qkf = qk[:, :, :].rearrange("p a t -> p (a t)")
        scores = qkf.rearrange("p (i a c n) -> p i a c n", i=TT, a=PH, c=2)
        scores_g = qkf.rearrange("p (g c n) -> p g c n", g=GROUPS, c=2)
        URING, VRING = 8, 4
        u_rows = ymix[:, :, :].rearrange("p a t -> p (a t)").rearrange("p (s d) -> p s d", s=URING)
        v_rows = wring[:, 0:VRING, :, :].rearrange("p s k n -> p s (k n)")

        bank_done = [sem(f"bank_done{b}") for b in range(BANKS)]
        bank_free = [sem(f"bank_free{b}") for b in range(BANKS)]
        w_ready = [sem(f"w_ready{s}") for s in range(RING)]
        x_in = [sem(f"x_in{i}") for i in range(TT)]
        par_in, keys_in, mem_in, gffn_in, gfin_in = (
            sem(n) for n in ("par_in", "keys_in", "mem_in", "gffn_in", "gfin_in"))
        consts = sem("consts")
        pads = sem("pads")
        cols_rdy = sem("cols_rdy")
        sq_done = sem("sq_done")
        eps_done = sem("eps_done")
        rms_done = sem("rms_done")
        xn_done = sem("xn_done")
        x3_done = sem("x3_done")
        z_done = sem("z_done")
        zs_done = sem("zs_done")
        zc_done = sem("zc_done")
        ez_done = sem("ez_done")
        ln_done = sem("ln_done")
        sp_done = sem("sp_done")
        spm_done = sem("spm_done")
        hi_done = sem("hi_done")
        lo_done = sem("lo_done")
        c_done = sem("c_done")
        arg_done = sem("arg_done")
        argm_done = sem("argm_done")
        wt_done = sem("wt_done")
        y_done = sem("y_done")
        y_out = sem("y_out")
        cu_done = sem("cu_done")
        gs_done = sem("gs_done")
        ga_done = sem("ga_done")
        xm_done = sem("xm_done")
        xp_done = sem("xp_done")
        h_done = sem("h_done")
        sc_out = sem("sc_out")
        tk = sem("tk")
        best_rdy = sem("best_rdy")
        idx_rdy = sem("idx_rdy")
        idx_cp = sem("idx_cp")
        slot_ok = sem("slot_ok")
        gate_rdy = sem("gate_rdy")
        u_ready = [sem(f"u_ready{s}") for s in range(URING)]
        v_ready = [sem(f"v_ready{s}") for s in range(VRING)]
        u_used = sem("u_used")
        v_free = sem("v_free")
        xc_done = sem("xc_done")
        gl_done = sem("gl_done")
        gle_done = sem("gle_done")
        wgt_rdy = sem("wgt_rdy")
        diag_rdy = sem("diag_rdy")
        acc_free = sem("acc_free")
        hadd = sem("hadd")
        fin_done = sem("fin_done")
        out_done = [sem(f"out_done{b}") for b in range(2)]

        whi_done = sem("whi_done")
        wlo_done = sem("wlo_done")
        w_half = sem("w_half")
        ahi_done = sem("ahi_done")
        alo_done = sem("alo_done")

        A_WC = TT
        A_GA = A_WC + KT
        A_XQ = A_GA + 2 * KT
        A_END = A_XQ + TT
        split_jobs = [(J_QK + n, n // RING, n % RING) for n in range(2 * KT)]
        Q_WC = len(split_jobs)
        split_jobs += [(J_WC + m, B_WC, m) for m in range(KT)]
        Q_GA = len(split_jobs)
        split_jobs += [(J_GA + n, B_GA + n // RING, n % RING) for n in range(2 * KT)]
        Q_XQ = len(split_jobs)
        split_jobs += [(J_XQ + m, B_XQ, m) for m in range(KT)]

        block = ctx.enter_context(nc.Block())

        def wait_free(eng, job):
            if job >= BANKS:
                eng.wait_ge(bank_free[job % BANKS], job // BANKS)

        def wait_job(eng, job):
            eng.wait_ge(bank_done[job % BANKS], job // BANKS + 1)

        def wait_taken(eng, job):
            eng.wait_ge(bank_free[job % BANKS], job // BANKS + 1)

        def wait_all_taken(eng, upto):
            for job in range(upto - BANKS, upto):
                wait_taken(eng, job)

        @block.sync
        def _(sp):
            for i in range(TT):
                sp.dma_start(h[:, i, :], x[0, P * i:P * (i + 1), :]).then_inc(x_in[i], 16)
            for n, blk in enumerate(blocks):
                for s in range(HALF if n >= B_XOR else 0, RING):
                    w2, c, _ = blk[s]
                    if n:
                        wait_job(sp, blocks[n - 1][s][2])
                    sp.dma_start(wring[:, s, :, :],
                                 w2.rearrange("(k p) n -> p k n", p=P)[:, :, P * c:P * (c + 1)]).then_inc(w_ready[s], 16)
                if n == B_WO:
                    wait_all_taken(sp, J_GA)
                    sp.dma_start(mem_tok, mem[0].rearrange("(i p) d -> p i d", p=P)).then_inc(mem_in, 16)
                if n == B_XO:
                    sp.dma_start(g_ffn, norm_ffn[0].partition_broadcast(P)).then_inc(gffn_in, 16)
            wait_job(sp, job_kr(NQ - 1))
            sp.dma_start(g_fin, norm_final.partition_broadcast(P)).then_inc(gfin_in, 16)
            for i in range(TT):
                sp.wait_ge(fin_done, i + 1)
                sp.dma_start(out[0, P * i:P * (i + 1), :], xnb[i % 2]).then_inc(out_done[i % 2], 16)
            for b in range(2):
                sp.wait_ge(out_done[b], 16 * TT // 2)

        @block.gpsimd
        def _(pool):
            pool.memset(ident[:, :], 0.0).then_inc(consts, 1)
            pool.memset(ones[:, :], 1.0).then_inc(consts, 1)
            pool.memset(nmask[:, :], 0.0).then_inc(consts, 1)
            pool.memset(neg_half[:, :], -0.5).then_inc(consts, 1)
            pool.wait_ge(consts, 4)
            pool.affine_select(out=ident[:, :], in_=ident[:, :], compare_op=ALU.not_equal, fill=1.0, base=0,
                               pattern=[[-1, P]], channel_multiplier=1).then_inc(consts, 1)
            pool.affine_select(out=tri[:, :], in_=ones[:, :], compare_op=ALU.is_ge, fill=0.0, base=0,
                               pattern=[[-1, P]], channel_multiplier=1).then_inc(consts, 1)
            pool.affine_select(out=cmask[:, :], in_=ones[:, :], compare_op=ALU.is_gt, fill=0.0, base=0,
                               pattern=[[1, P]], channel_multiplier=-1).then_inc(consts, 1)
            pool.affine_select(out=nmask[:, :], in_=nmask[:, :], compare_op=ALU.is_gt, fill=-1.0e30, base=0,
                               pattern=[[1, P]], channel_multiplier=-1).then_inc(consts, 1)
            pool.tensor_copy(ones_r[:, :], ones[:, :]).then_inc(consts, 1)
            pool.iota(iota16[:, :], pattern=[[1, TOPK]], base=0, channel_multiplier=0,
                      allow_small_or_imprecise_dtypes=True).then_inc(consts, 1)

            def inverse_rms(lo, hi):
                for n in range(lo, hi):
                    pool.wait_ge(sq_done, n + 1)
                    pool.tensor_scalar(rms[:, n:n + 1], ms[:, n:n + 1], EPS, None, ALU.add).then_inc(eps_done, 1)
                    pool.wait_ge(eps_done, n + 1)
                    pool.tensor_tensor(rms[:, n:n + 1], rms[:, n:n + 1], neg_half[:, :],
                                       ALU.pow).then_inc(rms_done, 1)

            def gather(table, index, to, ready):
                pool.indirect_dma_start(out=to, out_offset=None, in_=table,
                                        in_offset=bass.IndirectOffsetOnAxis(ap=index, axis=0)).then_inc(ready, 16)

            inverse_rms(0, 2 * TT + MT + 1)
            pool.wait_ge(idx_rdy, 1)
            pool.sem_inc(acc_free, 2)
            for e in range(TOPK):
                if e >= URING:
                    pool.wait_ge(u_used, e - URING + 1)
                gather(peer_u[0], idx_u[:, 0, e:e + 1], u_rows[:, e % URING, :], u_ready[e % URING])
            wait_job(pool, job_f(NQ - 1))
            pool.sem_inc(v_free, VRING)

            def pair(i, last):
                for b in range(2):
                    with_u = not (last and b == 1)
                    pool.wait_ge(idx_rdy, i * 2 + (b + 1))
                    pool.sem_inc(slot_ok, 1)
                    pool.tensor_copy(idx_v[:, b, :], idx_u[:, b, :]).then_inc(idx_cp, 1)
                    pool.wait_ge(idx_cp, i * 2 + (b + 1))
                    pool.sem_inc(slot_ok, 1)
                    if with_u:
                        pool.wait_ge(idx_rdy, i * 2 + (b + 2))
                        pool.sem_inc(slot_ok, 1)
                    for e in range(TOPK):
                        if with_u:
                            pool.wait_ge(u_used, i * (2 * TOPK) + (TOPK * (b + 1) + e - URING + 1))
                            pool.sem_inc(slot_ok, 1)
                            gather(peer_u[0], idx_u[:, 1 - b, e:e + 1], u_rows[:, e % URING, :], u_ready[e % URING])
                        pool.wait_ge(v_free, i * (2 * TOPK) + (TOPK * b + e + 1))
                        pool.sem_inc(slot_ok, 1)
                        gather(peer_v[0], idx_v[:, b, e:e + 1], v_rows[:, e % VRING, :], v_ready[e % VRING])
                        if isinstance(i, int) and 2 * i + b == G_N and e == 5:
                            inverse_rms(2 * TT + MT + 1, 3 * TT + MT)

            for i in range(G_N // 2 + 1):
                pair(i, False)
            with pool.Fori(G_N // 2 + 1, PAIRS - 1) as i:
                pair(i, False)
            pair(PAIRS - 1, True)
            inverse_rms(3 * TT + MT, 4 * TT + MT)

        @block.tensor
        def _(pe):
            pe.wait_ge(consts, 9)

            def transposes(job, tiles):
                wait_free(pe, job)
                for n, t in enumerate(tiles):
                    mm = pe.transpose(jb[:, job % BANKS, P * n:P * (n + 1)], t, ident[:, :])
                mm.then_inc(bank_done[job % BANKS], 1)

            def norm_transposes(job, done, count, tiles, source):
                for i in range(tiles):
                    pe.wait_ge(done, count + i + 1)
                    for half in range(2):
                        transposes(job + 2 * i + half, [source(i)[:, P * k:P * (k + 1)]
                                                        for k in range(4 * half, 4 * half + 4)])

            def feature_job(job, blk, s, act, n, lo=0, hi=KT):
                if lo == 0:
                    pe.wait_ge(w_ready[s], 16 * (blk + 1))
                    wait_free(pe, job)
                for k in range(lo, hi):
                    mm = pe.matmul(jb[:, job % BANKS, 0:n], wring[:, s, k, :], act[:, k, :],
                                   start=(k == 0), stop=(k == KT - 1))
                if hi == KT:
                    mm.then_inc(bank_done[job % BANKS], 1)

            def split_job(q, a_hi, a_lo):
                job = split_jobs[q][0]
                wait_free(pe, job)
                for half in range(2):
                    pe.wait_ge(wlo_done, 2 * q + half + 1)
                    for k in range(KT // 2):
                        kk = KT // 2 * half + k
                        for p, (w, a) in enumerate(((w_hi, a_hi), (w_hi, a_lo), (w_lo, a_hi))):
                            mm = pe.matmul(jb[:, job % BANKS, :], w[:, half, k, :], a[:, kk, :],
                                           start=(kk == 0 and p == 0), stop=(kk == KT - 1 and p == 2))
                    mm.then_inc(bank_done[job % BANKS] if half else w_half, 1)

            def token_jobs(job, blk, act, tiles):
                for half in range(2):
                    for s in range(4 * half, 4 * half + 4):
                        pe.wait_ge(w_ready[s], 16 * (blk + 1))
                    for i in range(tiles):
                        j = job + tiles * half + i
                        wait_free(pe, j)
                        for k in range(KT):
                            mm = pe.matmul(jb[:, j % BANKS, :], act[:, k, P * i:P * (i + 1)],
                                           wring[:, 4 * half:4 * half + 4, k, :],
                                           start=(k == 0), stop=(k == KT - 1))
                        mm.then_inc(bank_done[j % BANKS], 1)

            pe.wait_ge(par_in, 64)
            pe.transpose(jb[:, 0, 0:NROW], rows[:, :], ident[0:NROW, 0:NROW]).then_inc(bank_done[0], 1)
            norm_transposes(J_NORM1, xn_done, 0, TT, lambda i: xnb[i % 2])
            pe.wait_ge(keys_in, 16)
            for n in range(4):
                transposes(J_KEYS + n, [keys_raw[:, 4 * n + c, :] for c in range(4)])

            wait_all_taken(pe, J_KEYS)
            pe.wait_ge(alo_done, A_WC)
            for n in range(2 * KT):
                split_job(n, xq_hi, xq_lo)
            token_jobs(J_V, 2, xT, TT)
            wait_all_taken(pe, J_MIX)

            def ab_cols(j, lo, n):
                o = OFF[j] + lo
                return ab[:, o // BANK, o % BANK:o % BANK + n]

            def head_scores(hd):
                m, r = hd // 2, DH * (hd % 2)
                for t in range(TT):
                    mm = pe.matmul(ab_cols(t, 0, WID[t]), kT[r:r + DH, m, P * t:P * (t + 1)],
                                   qT[r:r + DH, m, P * t:SEQ], start=True, stop=True)
                mm.then_inc(z_done, 1)

            head_scores(0)
            for hd in range(SBH):
                m, b, r = hd // 2, hd % 2, DH * (hd % 2)
                j = J_MIX + 4 * m + 2 * b
                s = 4 * (m % 2) + 2 * b
                if hd == 0:
                    feature_job(j, B_MIX + m // 2, s, xT, SEQ)
                pe.wait_ge(lo_done, hd + 1)
                for t in range(TT):
                    for tt in range(t, TT):
                        for part in (sp_hi, sp_lo):
                            mm = pe.matmul(ab_cols(t, P * (tt - t), WID[tt]), (tri if tt == t else ones_r)[:, :],
                                           part[:, OFF[tt]:OFF[tt] + WID[tt]], start=(tt == t and part is sp_hi),
                                           stop=(tt == TT - 1 and part is sp_lo))
                mm.then_inc(c_done, 1)
                feature_job(j + 1, B_MIX + m // 2, s + 1, xT, SEQ, 0, 2)
                if hd + 1 < SBH:
                    pe.wait_ge(arg_done, hd + 1)
                    head_scores(hd + 1)
                feature_job(j + 1, B_MIX + m // 2, s + 1, xT, SEQ, 2, KT)
                pe.wait_ge(wt_done, hd + 1)
                if hd:
                    pe.wait_ge(y_out, hd)
                for t in range(TT):
                    mm = pe.matmul(ab[r:r + DH, 3, P * t:SEQ], vbuf[:, t, P * m + r:P * m + r + DH],
                                   wbuf[:, OFF[t]:OFF[t] + WID[t]], start=(t == 0), stop=(t == TT - 1))
                mm.then_inc(y_done, 1)
                if hd + 1 < SBH:
                    n = 2 * (hd + 1)
                    feature_job(J_MIX + n, B_MIX + n // RING, n % RING, xT, SEQ)

            pe.wait_ge(alo_done, A_GA)
            for m in range(KT):
                split_job(Q_WC + m, yc_hi, yc_lo)
            pe.wait_ge(alo_done, A_XQ)
            for m in range(KT):
                split_job(Q_GA + 2 * m, xg_hi, xg_lo)
                split_job(Q_GA + 2 * m + 1, ya_hi, ya_lo)
            pe.wait_ge(ga_done, 3 * KT)
            token_jobs(J_WO, B_WO, merged, TT)

            norm_transposes(J_MEMT, xn_done, TT, MT, lambda i: xnb[i % 2])
            wait_all_taken(pe, J_XK)
            for m in range(KT):
                feature_job(J_XK + m, B_XK, m, memT, M)
            token_jobs(J_XV, B_XV, memT, MT)

            norm_transposes(J_NORM2, xn_done, TT + MT, TT, lambda i: xnb[i % 2])
            wait_all_taken(pe, J_XQ)
            pe.wait_ge(alo_done, A_END)
            for m in range(KT):
                split_job(Q_XQ + m, xc_hi, xc_lo)
            wait_all_taken(pe, J_S)

            def cross_scores(i, half):
                j = job_s(i) + half
                wait_free(pe, j)
                for hh in range(2):
                    for k in range(2):
                        kt = 2 * (2 * half + hh) + k
                        mm = pe.matmul(jb[:, j % BANKS, M * hh:M * (hh + 1)], qT[:, kt, P * i:P * (i + 1)],
                                       memk[:, kt, :], start=(k == 0), stop=(k == 1))
                mm.then_inc(bank_done[j % BANKS], 1)

            def cross_probs(i, src):
                pe.wait_ge(xp_done, 2 * (i + 1))
                for mb in range(MT):
                    transposes(job_p(i) + mb, [src[:, M * hx + P * mb:M * hx + P * (mb + 1)] for hx in range(XH)])

            def cross_output(j, m, probsT, n):
                wait_free(pe, j)
                for mb in range(MT):
                    mm = pe.matmul(jb[:, j % BANKS, 0:n], memv[:, mb, P * m:P * (m + 1)], probsT[:, mb, m // 2, :],
                                   start=(mb == 0), stop=(mb == MT - 1))
                mm.then_inc(bank_done[j % BANKS], 1)

            for half in range(2):
                cross_scores(0, half)
            cross_probs(0, xnb[0])
            wait_all_taken(pe, J_O)
            for m in range(KT):
                cross_output(J_O + m, m, probs0T, P)
            wait_all_taken(pe, J_XO)
            token_jobs(J_XO, B_XO, oT, 1)

            norm_transposes(J_NORM3, x3_done, 0, 1, lambda i: vbuf[:, i, :])
            wait_all_taken(pe, J_PQ)

            def key_scores(j, q_job, c, tiles):
                wait_free(pe, j)
                wait_taken(pe, q_job)
                for i in range(tiles):
                    mm = pe.matmul(jb[:, j % BANKS, P * (tiles - 1 - i):P * (tiles - i)],
                                   q3[:, c % 2, P * i:P * (i + 1)], keysT[:, c, :], start=True, stop=True)
                mm.then_inc(bank_done[j % BANKS], 1)

            for c in range(NQ):
                feature_job(job_f(c), B_PQ + c // RING, c % RING, xT[:, :, 0:P], P)
                if c:
                    key_scores(job_k(c - 1), job_f(c - 1), c - 1, 1)
            key_scores(job_k(NQ - 1), job_f(NQ - 1), NQ - 1, 1)

            def weighted_rows(i, b, chore=None):
                pe.wait_ge(acc_free, i * 2 + (b + 1))
                for e in range(TOPK):
                    pe.wait_ge(diag_rdy, i * (2 * TOPK) + (TOPK * b + e + 1))
                    pe.wait_ge(v_ready[e % VRING], i * (2 * TOPK // VRING * 16)
                               + 16 * (TOPK // VRING * b + e // VRING + 1))
                    for c in range(2):
                        mm = pe.matmul(ab[:, 2 * b + c, :], diag[:, e, :],
                                       v_rows[:, e % VRING, BANK * c:BANK * (c + 1)],
                                       start=(e == 0), stop=(e == TOPK - 1))
                    mm.then_inc(v_free, 1)
                    if chore:
                        chore(e)

            def rest_step(g, e):
                if g == G_S and e < 5 * (TT - 1):
                    i = 1 + e // 5
                    if e % 5 < 2:
                        cross_scores(i, e % 5)
                    elif e % 5 == 4:
                        cross_probs(i, probs_tok)
                elif g == G_O and e < 4:
                    if e == 0:
                        wait_all_taken(pe, J_OR)
                    for m in (2 * e, 2 * e + 1):
                        cross_output(J_OR + m, m, probsRT, REST)
                elif g in (G_O, G_O + 1) and e >= 4:
                    half, i, k0 = g - G_O, e // 4, 2 * (e % 4)
                    j = J_XOR + (TT - 1) * half + i - 1
                    if k0 == 0:
                        if g == G_O and i == 1:
                            wait_all_taken(pe, J_XOR)
                        if i == 1:
                            for s in range(HALF, RING):
                                pe.wait_ge(w_ready[s], 16 * (B_XOR + half + 1))
                        wait_free(pe, j)
                    for k in (k0, k0 + 1):
                        mm = pe.matmul(jb[:, j % BANKS, :], oT[:, k, P * i:P * (i + 1)], wring[:, HALF:RING, k, :],
                                       start=(k == 0), stop=(k == KT - 1))
                    if k == KT - 1:
                        mm.then_inc(bank_done[j % BANKS], 1)
                elif g == G_N and e >= 10:
                    i, half = 1 + (e - 10) // 2, e % 2
                    pe.wait_ge(x3_done, i + 1)
                    transposes(J_NORM3R + e - 10, [vbuf[:, i, P * k:P * (k + 1)] for k in range(4 * half, 4 * half + 4)])
                elif g >= G_PQ:
                    a = g - G_PQ
                    if a == 0 and e == 0:
                        wait_all_taken(pe, J_PQR)
                    if a and e < 2:
                        c = 2 * a - 2 + e
                        key_scores(job_kr(c), job_fr(c), c, TT - 1)
                    c, k = 2 * a + e // KT, e % KT
                    feature_job(job_fr(c), B_PQR + c // HALF, HALF + c % HALF, xT[:, :, P:SEQ], REST, k, k + 1)

            for g in range(G_END):
                weighted_rows(g // 2, g % 2, lambda e, g=g: rest_step(g, e))
            for c in (NQ - 2, NQ - 1):
                key_scores(job_kr(c), job_fr(c), c, TT - 1)
            with pe.Fori(G_END // 2, PAIRS) as i:
                for b in range(2):
                    weighted_rows(i, b)

        XSCALE = float(XD) ** -0.5

        def take_probs(act, i):
            for mb in range(MT):
                j = job_p(i) + mb
                wait_job(act, j)
                act.activation(probs0T[:, mb, :, :] if i == 0 else probsRT[:, mb, :, P * (i - 1):P * i],
                               jb[:, j % BANKS, :].rearrange("p (h t) -> p h t", h=XH),
                               ACT.Copy).then_inc(bank_free[j % BANKS], 1)

        def gate_exp(act, g, b):
            act.wait_ge(best_rdy, g + 1)
            act.activation(gate_e[:, b, :], best[:, b, :], ACT.Exp, bias=neg_best[:, b:b + 1],
                           accum_out=gate_s[:, b:b + 1]).then_inc(gate_rdy, 1)

        @block.scalar
        def _(act):
            for n, src in enumerate((norm_mix, norm_xattn, norm_mem)):
                act.dma_start(rows[KT * n:KT * (n + 1), :], src[0].rearrange("(k p) -> k p", p=P)).then_inc(par_in, 16)
            act.dma_start(rows[3 * KT:NROW, :], conv_w[0].rearrange("c (k p) -> (c k) p", p=P)).then_inc(par_in, 16)
            act.dma_start(keys_raw, peer_sub_keys[0].rearrange("h c n d -> n (h c) d")).then_inc(keys_in, 16)

            def mean_square(src, n):
                if n:
                    act.wait_ge(sq_done, n)
                act.activation(sp_hi[:, 0:D], src, ACT.Square,
                               scale=float(D) ** -0.5, accum_out=ms[:, n:n + 1]).then_inc(sq_done, 1)

            def normed(src, n, slot):
                act.wait_ge(rms_done, n + 1)
                act.activation(xnb[slot], src, ACT.Copy, scale=rms[:, n:n + 1]).then_inc(xn_done, 1)

            def high_part(src, to):
                act.activation(to, src, ACT.Copy).then_inc(ahi_done, 1)

            def high_weights(q, halves=(0, 1)):
                job, blk, s = split_jobs[q]
                for half in halves:
                    act.wait_ge(w_ready[s], 16 * (blk + 1))
                    if q and half == 0:
                        act.wait_ge(w_half, q)
                    elif q:
                        wait_job(act, split_jobs[q - 1][0])
                    act.activation(w_hi[:, half, :, :], wring[:, s, KT // 2 * half:KT // 2 * (half + 1), :],
                                   ACT.Copy).then_inc(whi_done, 1)

            def x_high(i, job, to):
                for half in range(2):
                    wait_taken(act, job + 2 * i + half)
                high_part(xT[:, :, P * i:P * (i + 1)], to[:, :, P * i:P * (i + 1)])

            for i in range(TT):
                act.wait_ge(x_in[i], 16)
                mean_square(h[:, i, :], i)
                if i >= 2:
                    wait_job(act, J_NORM1 + 2 * (i - 2) + 1)
                normed(h[:, i, :], i, i % 2)
                if i:
                    x_high(i - 1, J_NORM1, xq_hi)
            high_weights(0)
            x_high(TT - 1, J_NORM1, xq_hi)

            def take(job, to, n=BANK, **kw):
                wait_job(act, job)
                act.activation(to, jb[:, job % BANKS, 0:n], kw.get("func", ACT.Copy),
                               scale=kw.get("scale", 1.0)).then_inc(bank_free[job % BANKS], 1)

            for n in range(2 * KT):
                if n + 1 < 2 * KT:
                    high_weights(n + 1)
                take(J_QK + n, qk[:, n, :])
            for half in range(2):
                for i in range(TT):
                    take(J_V + TT * half + i, vbuf[:, i, BANK * half:BANK * (half + 1)])

            for hd in range(SBH + 1):
                m, b = hd // 2, hd % 2
                if hd < SBH:
                    act.wait_ge(zc_done, hd + 1)
                    act.activation(spb, spb, ACT.Exp).then_inc(ez_done, 1)
                    act.wait_ge(ez_done, hd + 1)
                    act.activation(spb, spb, ACT.Ln, bias=1.0).then_inc(ln_done, 1)
                if hd:
                    r = DH * (1 - b)
                    act.wait_ge(y_done, hd)
                    act.activation(qT[r:r + DH, (hd - 1) // 2, :], ab[r:r + DH, 3, :], ACT.Copy).then_inc(y_out, 1)
                    if b == 0:
                        take(J_MIX + 2 * hd - 1, merged[:, m - 1, :], func=ACT.Exp, scale=-1.0)
                if hd < SBH:
                    act.wait_ge(spm_done, hd + 1)
                    act.activation(sp_hi[:, :], spb, ACT.Copy).then_inc(hi_done, 1)
                    act.wait_ge(argm_done, hd + 1)
                    act.activation(wbuf, zs, ACT.Exp).then_inc(wt_done, 1)
                    if b == 0:
                        if m:
                            wait_taken(act, J_MIX + 4 * (m - 1) + 1)
                        take(J_MIX + 4 * m, cxs[:, :])
                        if m:
                            wait_taken(act, J_MIX + 4 * (m - 1) + 2)
                            high_part(yconv[:, m - 1, :], yc_hi[:, m - 1, :])

            high_weights(Q_WC)
            wait_taken(act, J_MIX + 4 * (KT - 1) + 2)
            high_part(yconv[:, KT - 1, :], yc_hi[:, KT - 1, :])
            for m in range(KT):
                if m + 1 < KT:
                    high_weights(Q_WC + m + 1)
                high_part(xT[:, m, :], xg_hi[:, m, :])
                high_part(qT[:, m, :], ya_hi[:, m, :])
            high_weights(Q_GA)
            for m in range(KT):
                high_weights(Q_GA + 2 * m + 1)
                if m >= 2:
                    act.wait_ge(ga_done, 3 * (m - 1))
                take(J_GA + 2 * m, gex[:, m % 2, :], func=ACT.Exp, scale=-1.0)
                if m + 1 < KT:
                    high_weights(Q_GA + 2 * m + 2)

            act.wait_ge(mem_in, 16)
            wait_job(act, J_WO - 1)
            for i in range(MT):
                mean_square(mem_tok[:, i, :], TT + i)
                normed(mem_tok[:, i, :], TT + i, i % 2)
            for m in range(KT):
                take(J_XK + m, memk[:, m, :], n=M)
            for half in range(2):
                for i in range(MT):
                    take(J_XV + MT * half + i, memv[:, i, BANK * half:BANK * (half + 1)])

            wait_all_taken(act, J_MEMT)
            for i in range(TT):
                mean_square(h[:, i, :], TT + MT + i)
                if i >= 2:
                    wait_job(act, J_NORM2 + 2 * (i - 2) + 1)
                else:
                    wait_job(act, J_MEMT + 2 * MT - 1)
                normed(h[:, i, :], TT + MT + i, i % 2)
                if i:
                    x_high(i - 1, J_NORM2, xc_hi)
            high_weights(Q_XQ)
            x_high(TT - 1, J_NORM2, xc_hi)
            for m in range(KT):
                if m + 1 < KT:
                    high_weights(Q_XQ + m + 1)
                take(J_XQ + m, qT[:, m, :])
            def exp_scores(i, to):
                act.wait_ge(xm_done, 2 * (i + 1))
                wait_job(act, job_p(i - 1) + 1 if i else J_XQ - 1)
                for hx in range(XH):
                    j = job_s(i) + hx // 2
                    ex = act.activation(to[:, M * hx:M * (hx + 1)],
                                        jb[:, j % BANKS, M * (hx % 2):M * (hx % 2 + 1)], ACT.Exp,
                                        scale=XSCALE, bias=xneg[:, i, hx:hx + 1], accum_out=xsum[:, i, hx:hx + 1])
                    if hx % 2:
                        ex.then_inc(bank_free[j % BANKS], 1)

            exp_scores(0, xnb[0])
            take_probs(act, 0)
            for m in range(KT):
                take(J_O + m, oT[:, m, 0:P], n=P)
            wait_taken(act, J_XO + 1)
            mean_square(h[:, 0, :], 2 * TT + MT)

            def take_key_scores(j, c, lo, hi, scored):
                wait_job(act, j)
                act.activation(scores[:, TT - hi:TT - lo, PH - 1 - c // 2, c % 2, :],
                               jb[:, j % BANKS, 0:P * (hi - lo)].rearrange("p (i n) -> p i n", i=hi - lo),
                               ACT.Copy).then_inc(bank_free[j % BANKS], 1)
                wait_taken(act, j)
                act.sem_inc(sc_out, scored)

            for c in range(NQ):
                if c >= 2:
                    wait_job(act, job_k(c - 2))
                take(job_f(c), q3[:, c % 2, 0:P], n=P)
                if c:
                    take_key_scores(job_k(c - 1), c - 1, 0, 1, 1)
                if c in (6, 10):
                    gate_exp(act, (c - 6) // 4, (c - 6) // 4)
            take_key_scores(job_k(NQ - 1), NQ - 1, 0, 1, 1)

            def take_rest(g):
                if g == G_S:
                    for i in range(1, TT):
                        exp_scores(i, probs_tok)
                        take_probs(act, i)
                elif g == G_O:
                    for m in range(KT):
                        take(J_OR + m, oT[:, m, P:SEQ], n=REST)
                elif g == G_N:
                    for i in range(1, TT):
                        wait_taken(act, J_XOR + TT - 1 + i - 1)
                        mean_square(h[:, i, :], 2 * TT + MT + i)
                elif g >= G_PQ:
                    if g > G_PQ:
                        take_rest_scores(g - G_PQ - 1)
                    if g < G_END:
                        take_rest_queries(g - G_PQ)

            def take_rest_scores(g):
                for c in (2 * g, 2 * g + 1):
                    take_key_scores(job_kr(c), c, 1, TT, 1 if c < NQ - 1 else 2 * GROUPS - 2 * NQ + 1)

            def take_rest_queries(g):
                for c in (2 * g, 2 * g + 1):
                    wait_job(act, job_kr(c - 2) if g else job_k(NQ - 2 + c))
                    take(job_fr(c), q3[:, c % 2, 0:REST], n=REST)

            def pair(i, first, last):
                for b in range(2):
                    act.wait_ge(gl_done, i * 16 + (8 * b + 4))
                    act.activation(gl[:, 2, :], gl[:, 1, :], ACT.Exp, scale=-GELU_C).then_inc(gle_done, 1)
                    act.wait_ge(wgt_rdy, i * 2 + (b + 1))
                    for e in range(TOPK):
                        if not (first and b == 0):
                            act.wait_ge(v_free, i * (2 * TOPK) + (TOPK * (b - 1) + e + 1 + VRING))
                        act.activation(diag[:, e, :], ident[:, :], ACT.Copy,
                                       scale=wgt[:, b, e:e + 1]).then_inc(diag_rdy, 1)
                    if isinstance(i, int) and 2 * i + b < G_END:
                        take_rest(2 * i + b)
                    if not last:
                        gate_exp(act, i * 2 + (b + 2), b)

            for i in range(G_END // 2):
                pair(i, i == 0, False)
            take_rest(G_END)
            with act.Fori(G_END // 2, PAIRS - 1) as i:
                pair(i, False, False)
            pair(PAIRS - 1, False, True)

            for i in range(TT):
                act.wait_ge(hadd, 1)
                mean_square(h[:, i, :], 3 * TT + MT + i)

        @block.vector
        def _(dve):
            dve.memset(u_pad[:, :], 0.0).then_inc(pads, 1)

            wait_job(dve, J_PARAM)
            dve.tensor_copy(cols[:, :], jb[:, 0, 0:NROW]).then_inc(bank_free[0], 1)
            wait_taken(dve, J_PARAM)

            def take_normed(job, i, to, g0):
                for half in range(2):
                    j = job + 2 * i + half
                    wait_job(dve, j)
                    src = jb[:, j % BANKS, :].rearrange("p (k t) -> p k t", k=4)
                    dst = to[:, 4 * half:4 * half + 4, P * i:P * (i + 1)]
                    if g0 is None:
                        dve.tensor_copy(dst, src).then_inc(bank_free[j % BANKS], 1)
                    else:
                        gain = cols[:, g0 + 4 * half:g0 + 4 * half + 4].unsqueeze(2).to_broadcast([P, 4, P])
                        dve.tensor_tensor(dst, src, gain, ALU.mult).then_inc(bank_free[j % BANKS], 1)

            def low_part(n, src, high, to):
                dve.wait_ge(ahi_done, n + 1)
                dve.tensor_tensor(to, src, high, ALU.subtract).then_inc(alo_done, 1)

            def low_weights(q):
                s = split_jobs[q][2]
                for half in range(2):
                    dve.wait_ge(whi_done, 2 * q + half + 1)
                    dve.tensor_tensor(w_lo[:, half, :, :], wring[:, s, KT // 2 * half:KT // 2 * (half + 1), :],
                                      w_hi[:, half, :, :], ALU.subtract).then_inc(wlo_done, 1)

            def x_low(n, i, hi, lo):
                t = slice(P * i, P * (i + 1))
                low_part(n, xT[:, :, t], hi[:, :, t], lo[:, :, t])

            for i in range(TT + 1):
                if i < TT:
                    take_normed(J_NORM1, i, xT, 0)
                if i:
                    if i == TT:
                        low_weights(0)
                    x_low(i - 1, i - 1, xq_hi, xq_lo)
            for n in range(4):
                j = J_KEYS + n
                wait_job(dve, j)
                dve.tensor_copy(keysT[:, 4 * n:4 * n + 4, :],
                                jb[:, j % BANKS, :].rearrange("p (c n) -> p c n", c=4)).then_inc(bank_free[j % BANKS], 1)
            dve.memset(zs[:, OFF[1] + WID[1]:OFF[2]], 0.0).then_inc(pads, 1)
            dve.memset(spb[:, OFF[1] + WID[1]:OFF[2]], 0.0).then_inc(pads, 1)
            dve.wait_ge(pads, 3)
            for q in range(1, 2 * KT):
                low_weights(q)

            z_parts = [(ab[:, 0, :], lambda t: t[:, 0:BANK]),
                       (ab[:, 1, 0:WID[1]], lambda t: t[:, OFF[1]:OFF[1] + WID[1]]),
                       (ab[:, 2, 0:WID[1]], lambda t: t[:, OFF[2]:OFF[2] + WID[1]])]

            def diagonal(t, op, mask, done):
                for n in range(TT):
                    d = t[:, OFF[n]:OFF[n] + P]
                    last = dve.tensor_tensor(d, d, mask[:, :], op)
                last.then_inc(done, 1)

            def sigmoid_tail(m):
                wait_taken(dve, J_MIX + 4 * m + 3)
                dve.tensor_scalar(merged[:, m, :], merged[:, m, :], 1.0, None, ALU.add).then_inc(gs_done, 1)
                dve.wait_ge(gs_done, 2 * m + 1)
                dve.reciprocal(merged[:, m, :], merged[:, m, :]).then_inc(gs_done, 1)

            def convolve(m):
                j = J_MIX + 4 * m + 1
                wait_job(dve, j)
                wait_taken(dve, j - 1)
                dve.tensor_tensor(u_pad[:, CONVK - 1:], jb[:, j % BANKS, :], cxs[:, :],
                                  ALU.mult).then_inc(bank_free[j % BANKS], 1)
                wait_taken(dve, j)
                for c in range(CONVK):
                    tap = cols[:, KT * (3 + c) + m:KT * (3 + c) + m + 1]
                    if c == 0:
                        if m:
                            wait_taken(dve, J_MIX + 4 * (m - 1) + 2)
                        st = dve.tensor_scalar(ytap[:, :], u_pad[:, 0:SEQ], tap, None, ALU.mult)
                    else:
                        dve.wait_ge(cu_done, 3 * m + c)
                        st = dve.scalar_tensor_tensor(out=ytap[:, :], in0=u_pad[:, c:c + SEQ], scalar=tap,
                                                      in1=ytap[:, :], op0=ALU.mult, op1=ALU.add)
                    st.then_inc(cu_done, 1)

            def gate_convolved(m):
                j = J_MIX + 4 * m + 2
                wait_job(dve, j)
                dve.wait_ge(cu_done, 3 * (m + 1))
                dve.tensor_tensor(yconv[:, m, :], jb[:, j % BANKS, :], ytap[:, :],
                                  ALU.mult).then_inc(bank_free[j % BANKS], 1)

            for hd in range(SBH):
                m, b = hd // 2, hd % 2
                dve.wait_ge(z_done, hd + 1)
                if hd:
                    dve.wait_ge(wt_done, hd)
                for ps, part in z_parts:
                    last = dve.tensor_scalar(part(zs), ps, float(DH) ** -0.5, None, ALU.mult)
                last.then_inc(zs_done, 1)
                dve.wait_ge(zs_done, hd + 1)
                dve.tensor_scalar(spb, zs, SP_CAP, None, ALU.min).then_inc(zc_done, 1)
                if m and b:
                    sigmoid_tail(m - 1)
                    low_part(A_WC + m - 1, yconv[:, m - 1, :], yc_hi[:, m - 1, :], yc_lo[:, m - 1, :])
                elif m:
                    convolve(m - 1)
                dve.wait_ge(ln_done, hd + 1)
                dve.tensor_tensor(spb, spb, zs, ALU.max).then_inc(sp_done, 1)
                dve.wait_ge(sp_done, hd + 1)
                diagonal(spb, ALU.mult, cmask, spm_done)
                dve.wait_ge(hi_done, hd + 1)
                dve.tensor_tensor(sp_lo[:, :], spb, sp_hi[:, :], ALU.subtract).then_inc(lo_done, 1)
                dve.wait_ge(c_done, hd + 1)
                for ps, part in z_parts:
                    last = dve.tensor_tensor(part(zs), part(zs), ps, ALU.subtract)
                last.then_inc(arg_done, 1)
                dve.wait_ge(arg_done, hd + 1)
                diagonal(zs, ALU.min, nmask, argm_done)
                if m and b == 0:
                    gate_convolved(m - 1)
            convolve(KT - 1)
            gate_convolved(KT - 1)
            low_weights(Q_WC)
            low_part(A_WC + KT - 1, yconv[:, KT - 1, :], yc_hi[:, KT - 1, :], yc_lo[:, KT - 1, :])
            sigmoid_tail(KT - 1)

            for m in range(KT):
                j = J_WC + m
                if m + 1 < KT:
                    low_weights(Q_WC + m + 1)
                low_part(A_GA + 2 * m, xT[:, m, :], xg_hi[:, m, :], xg_lo[:, m, :])
                low_part(A_GA + 2 * m + 1, qT[:, m, :], ya_hi[:, m, :], ya_lo[:, m, :])
                wait_job(dve, j)
                dve.wait_ge(gs_done, 2 * (m + 1))
                dve.tensor_tensor(merged[:, m, :], jb[:, j % BANKS, :], merged[:, m, :],
                                  ALU.mult).then_inc(bank_free[j % BANKS], 1)
            low_weights(Q_GA)
            for m in range(KT):
                j = J_GA + 2 * m
                gx = gex[:, m % 2, :]
                low_weights(Q_GA + 2 * m + 1)
                wait_taken(dve, j)
                dve.tensor_scalar(gx, gx, 1.0, None, ALU.add).then_inc(ga_done, 1)
                dve.wait_ge(ga_done, 3 * m + 1)
                dve.reciprocal(gx, gx).then_inc(ga_done, 1)
                if m + 1 < KT:
                    low_weights(Q_GA + 2 * m + 2)
                dve.wait_ge(ga_done, 3 * m + 2)
                wait_job(dve, j + 1)
                dve.tensor_tensor(gx, jb[:, (j + 1) % BANKS, :], gx, ALU.mult).then_inc(bank_free[(j + 1) % BANKS], 1)
                wait_taken(dve, j + 1)
                wait_taken(dve, J_WC + m)
                dve.tensor_tensor(merged[:, m, :], merged[:, m, :], gx, ALU.add).then_inc(ga_done, 1)

            def residual(job):
                for half in range(2):
                    for i in range(TT):
                        j = job + TT * half + i
                        wait_job(dve, j)
                        hh = h[:, i, BANK * half:BANK * (half + 1)]
                        dve.tensor_tensor(hh, jb[:, j % BANKS, :], hh, ALU.add).then_inc(bank_free[j % BANKS], 1)

            residual(J_WO)
            for i in range(MT + 1):
                if i:
                    take_normed(J_MEMT, i - 1, memT, 2 * KT)
            for i in range(TT + 1):
                if i < TT:
                    take_normed(J_NORM2, i, xT, KT)
                if i:
                    if i == TT:
                        low_weights(Q_XQ)
                    x_low(A_XQ + i - 1, i - 1, xc_hi, xc_lo)
            for m in range(1, KT):
                low_weights(Q_XQ + m)

            def row_maxima(i):
                for half in range(2):
                    j = job_s(i) + half
                    wait_job(dve, j)
                    rd = dve.tensor_reduce(xmax[:, i, 2 * half:2 * half + 2],
                                           jb[:, j % BANKS, :].rearrange("p (h m) -> p h m", h=2), AX.X, ALU.max)
                rd.then_inc(xm_done, 1)
                dve.wait_ge(xm_done, 2 * i + 1)
                dve.tensor_scalar(xneg[:, i, :], xmax[:, i, :], -XSCALE, None, ALU.mult).then_inc(xm_done, 1)

            def probabilities(i, tok):
                for half in range(2):
                    wait_taken(dve, job_s(i) + half)
                dve.reciprocal(xinv[:, i, :], xsum[:, i, :]).then_inc(xp_done, 1)
                dve.wait_ge(xp_done, 2 * i + 1)
                pr = tok.rearrange("p (h m) -> p h m", h=XH)
                dve.tensor_tensor(pr, pr, xinv[:, i, :].unsqueeze(2).to_broadcast([P, XH, M]),
                                  ALU.mult).then_inc(xp_done, 1)

            def add_output(j, i, half):
                wait_job(dve, j)
                hh = h[:, i, BANK * half:BANK * (half + 1)]
                dve.tensor_tensor(hh, jb[:, j % BANKS, :], hh, ALU.add).then_inc(bank_free[j % BANKS], 1)

            def norm_tile(i):
                n = 2 * TT + MT + i
                dve.wait_ge(rms_done, n + 1)
                dve.scalar_tensor_tensor(out=vbuf[:, i, :], in0=h[:, i, :], scalar=rms[:, n:n + 1], in1=g_ffn,
                                         op0=ALU.mult, op1=ALU.mult).then_inc(x3_done, 1)

            row_maxima(0)
            probabilities(0, xnb[0])
            for half in range(2):
                add_output(J_XO + half, 0, half)
            dve.wait_ge(gffn_in, 16)
            norm_tile(0)
            take_normed(J_NORM3, 0, xT, None)

            def rest_step(g, e):
                if g == G_S and e < 5 * (TT - 1):
                    if e % 5 == 1:
                        row_maxima(1 + e // 5)
                    elif e % 5 == 2:
                        probabilities(1 + e // 5, probs_tok)
                if g in (G_O, G_O + 1) and e in (9, 13) or g in (G_O + 1, G_O + 2) and e == 1:
                    n = (e - 9) // 4 if e > 1 else 2
                    half = g - G_O - (e == 1)
                    add_output(J_XOR + (TT - 1) * half + n, 1 + n, half)
                if g == G_N and e in (8, 9, 10):
                    norm_tile(e - 7)
                if g == G_N and e >= 13:
                    take_normed(J_NORM3R, e - 13, xT[:, :, P:SEQ], None)

            def select(g, b):
                n = [0]

                def after(ins):
                    ins.then_inc(tk, 1)
                    n[0] += 1
                    dve.wait_ge(tk, n[0])

                def top16(vals, src, where):
                    after(dve.max(vals[:, 0:8], src))
                    after(dve.max_index(where[:, 0:8], vals[:, 0:8], src))
                    after(dve.match_replace(src, vals[:, 0:8], src, LOWEST))
                    after(dve.max(vals[:, 8:16], src))
                    after(dve.max_index(where[:, 8:16], vals[:, 8:16], src))

                dve.wait_ge(sc_out, g * 2 + 2)
                after(dve.tensor_copy(cur[:, :, :], scores_g[:, GROUPS - 1 - g, :, :] if isinstance(g, int)
                                      else scores_g[:, bass.ds(g * -1 + (GROUPS - 1), 1), :, :]
                                      .rearrange("p g c n -> p (g c) n")))
                for c in range(2):
                    top16(top_v[:, c, :], cur[:, c, :], top_i[:, c, :])
                candv = cand.rearrange("p (a b) -> p a b", a=TOPK)
                after(dve.tensor_tensor(candv, top_v[:, 0, :].unsqueeze(2).to_broadcast([P, TOPK, TOPK]),
                                        top_v[:, 1, :].unsqueeze(1).to_broadcast([P, TOPK, TOPK]), ALU.add))
                after(dve.tensor_scalar(top_f[:, 0, :], top_i[:, 0, :], float(NK), None, ALU.mult))
                after(dve.tensor_copy(top_f[:, 1, :], top_i[:, 1, :]))
                top16(best[:, b, :], cand, pos[:, :])
                dve.tensor_scalar(neg_best[:, b:b + 1], best[:, b, 0:1], -1.0, None, ALU.mult).then_inc(best_rdy, 1)
                after(dve.tensor_scalar(pos_ab[:, 0, :], pos[:, :], 4, None, ALU.logical_shift_right))
                after(dve.tensor_scalar(pos_ab[:, 1, :], pos[:, :], TOPK - 1, None, ALU.bitwise_and))
                after(dve.tensor_copy(pos_f[:, :, :], pos_ab[:, :, :]))
                for c in range(2):
                    after(dve.tensor_tensor(hot, pos_f[:, c, :].unsqueeze(2).to_broadcast([P, TOPK, TOPK]),
                                            iota16[:, :].unsqueeze(1).to_broadcast([P, TOPK, TOPK]), ALU.is_equal))
                    after(dve.tensor_tensor(hot, hot, top_f[:, c, :].unsqueeze(1).to_broadcast([P, TOPK, TOPK]),
                                            ALU.mult))
                    after(dve.tensor_reduce(sel[:, c, :], hot, AX.X, ALU.add))
                dve.sem_clear(tk)
                dve.tensor_tensor(idx_u[:, b, :], sel[:, 0, :], sel[:, 1, :], ALU.add).then_inc(idx_rdy, 1)

            dve.wait_ge(consts, 10)
            select(0, 0)
            select(1, 1)

            def tile_of(t, q):
                return t[:, q, :] if isinstance(q, int) else t[:, bass.ds(q, 1), :].rearrange("p a d -> p (a d)")

            def add_experts(i, b):
                dve.wait_ge(v_free, i * (2 * TOPK) + (TOPK * (b + 1) + VRING))
                hh = tile_of(h, i // (PH // 2))
                return dve.tensor_tensor(hh, ab[:, 2 * b:2 * b + 2, :].rearrange("p c n -> p (c n)"), hh, ALU.add)

            def pair(i, first, last):
                for b in range(2):
                    if b == 0:
                        dve.tensor_copy(xcur, tile_of(vbuf, i // (PH // 2))).then_inc(xc_done, 1)
                        dve.wait_ge(xc_done, i + 1)
                    for e in range(TOPK):
                        dve.wait_ge(u_ready[e % URING], i * (2 * TOPK // URING * 16)
                                    + 16 * (TOPK // URING * b + e // URING + 1))
                        u = u_rows[:, e % URING, :]
                        dve.tensor_tensor_reduce(out=u, in0=u, in1=xcur, scale=1.0, scalar=0.0, op0=ALU.mult,
                                                 op1=ALU.add, accum_out=dots[:, b, e:e + 1]).then_inc(u_used, 1)
                        if isinstance(i, int) and i + b > 0:
                            rest_step(2 * i + b - 1, e)
                    a = dots[:, b, :]
                    n = [0]

                    def step(ins):
                        ins.then_inc(gl_done, 1)
                        n[0] += 1

                    def wait_steps():
                        dve.wait_ge(gl_done, i * 16 + (8 * b + n[0]))

                    dve.wait_ge(u_used, i * (2 * TOPK) + TOPK * (b + 1))
                    step(dve.tensor_tensor(gl[:, 0, :], a, a, ALU.mult))
                    wait_steps()
                    step(dve.tensor_scalar(gl[:, 0, :], gl[:, 0, :], 0.044715, 1.0, ALU.mult, ALU.add))
                    wait_steps()
                    step(dve.tensor_tensor(gl[:, 1, :], gl[:, 0, :], a, ALU.mult))
                    wait_steps()
                    step(dve.tensor_scalar(gl[:, 1, :], gl[:, 1, :], GELU_FLOOR, None, ALU.max))
                    dve.wait_ge(gate_rdy, i * 2 + (b + 1))
                    step(dve.tensor_tensor(gl[:, 3, :], a, gate_e[:, b, :], ALU.mult))
                    step(dve.reciprocal(gate_r[:, b:b + 1], gate_s[:, b:b + 1]))
                    dve.wait_ge(gle_done, i * 2 + (b + 1))
                    step(dve.tensor_scalar(gl[:, 2, :], gl[:, 2, :], 1.0, None, ALU.add))
                    wait_steps()
                    step(dve.reciprocal(gl[:, 2, :], gl[:, 2, :]))
                    wait_steps()
                    if not first:
                        dve.wait_ge(diag_rdy, i * (2 * TOPK) + TOPK * (b - 1))
                    dve.scalar_tensor_tensor(out=wgt[:, b, :], in0=gl[:, 3, :], scalar=gate_r[:, b:b + 1],
                                             in1=gl[:, 2, :], op0=ALU.mult, op1=ALU.mult).then_inc(wgt_rdy, 1)
                    if not last:
                        dve.wait_ge(idx_cp, i * 2 + (b + 1))
                        select(i * 2 + (b + 2), b)
                    if not (first and b == 0):
                        add_experts(i - (1 - b), 1 - b).then_inc(acc_free, 1)

            for i in range(G_N // 2 + 2):
                pair(i, i == 0, False)
            with dve.Fori(G_N // 2 + 2, PAIRS - 1) as i:
                pair(i, False, False)
            pair(PAIRS - 1, False, True)
            dve.wait_ge(acc_free, 2 * PAIRS + 1)
            add_experts(PAIRS - 1, 1).then_inc(hadd, 1)

            dve.wait_ge(gfin_in, 16)
            for i in range(TT):
                n = 3 * TT + MT + i
                dve.wait_ge(rms_done, n + 1)
                if i >= 2:
                    dve.wait_ge(out_done[i % 2], 16 * (i // 2))
                dve.scalar_tensor_tensor(out=xnb[i % 2], in0=h[:, i, :], scalar=rms[:, n:n + 1], in1=g_fin,
                                         op0=ALU.mult, op1=ALU.mult).then_inc(fin_done, 1)


_INS = ["x", "mem", "norm_mix", "w_in", "conv_w", "w_branch_attn", "w_branch_conv", "w_out", "norm_xattn", "norm_mem",
        "xattn_wq", "xattn_wk", "xattn_wv", "xattn_wo", "norm_ffn", "peer_w_query", "peer_sub_keys", "peer_u",
        "peer_v", "norm_final"]


def kernel(**inputs):
    import numpy as _np
    import concourse.bacc as _bacc
    from concourse import mybir as _mybir
    from concourse.bass_utils import run_bass_kernel_spmd as _run

    nc = _bacc.Bacc("TRN2", target_bir_lowering=False, num_devices=1)
    arrays, args = {}, []
    for name in _INS:
        a = _np.ascontiguousarray(inputs[name])
        arrays[f"in_{name}_dram"] = a
        args.append(nc.dram_tensor(f"in_{name}_dram", a.shape, _mybir.dt.from_np(a.dtype), kind="ExternalInput").ap())
    shape = inputs["x"].shape
    args.append(nc.dram_tensor("out_0_dram", shape, _mybir.dt.float32, kind="ExternalOutput").ap())
    build_trunk(nc, *args)
    r = _run(nc, [arrays], core_ids=[0])
    return r.results[0]["out_0_dram"]
```

```python
from contextlib import ExitStack

import concourse.bass as bass
from concourse import mybir

F32 = mybir.dt.float32
U32 = mybir.dt.uint32
F32R = mybir.dt.float32r
ALU = mybir.AluOpType
ACT = mybir.ActivationFunctionType
AX = mybir.AxisListType

P = 128
BANK = 512
BANKS = 4
RING = 8
EPS = 1e-6
SP_CAP = 40.0
GELU_C = 2.0 * 0.7978845608028654
GELU_FLOOR = -50.0
LOWEST = -3.0e38


def build_trunk(nc, x, mem, norm_mix, w_in, conv_w, w_branch_attn, w_branch_conv, w_out,
                norm_xattn, norm_mem, xattn_wq, xattn_wk, xattn_wv, xattn_wo,
                norm_ffn, peer_w_query, peer_sub_keys, peer_u, peer_v, norm_final, out):
    D = x.shape[2]
    SEQ = x.shape[1]
    M = mem.shape[1]
    KT = D // P
    TT = SEQ // P
    MT = M // P
    SBH, DH = 16, 64
    XH, XD = 4, D // 4
    PH, NK, TOPK = peer_sub_keys.shape[1], peer_sub_keys.shape[3], 16
    CONVK = conv_w.shape[1]
    NROW = 3 * KT + CONVK * KT
    GROUPS = TT * PH
    PAIRS = GROUPS // 2
    assert SBH * DH == D and (KT, TT, MT, NK, TOPK, PH) == (8, 4, 2, 128, 16, 8)

    WID = [SEQ - P * j for j in range(TT)]
    OFF = [0, BANK, 2 * BANK, 2 * BANK + WID[2]]
    SPAN = OFF[3] + WID[3]

    COLQ, COLK, COLV, COLX, COLB, COLC, COLGA, COLGC = (KT * n for n in range(8))

    J_PARAM = 0
    J_NORM1 = J_PARAM + 1
    J_KEYS = J_NORM1 + 2 * TT
    J_QK = J_KEYS + 4
    J_V = J_QK + 2 * KT
    J_MIX = J_V + 2 * TT
    J_WC = J_MIX + 4 * KT
    J_GA = J_WC + KT
    J_MEMT = J_GA + 2 * KT
    J_WO = J_MEMT + 2 * MT
    J_XK = J_WO + 2 * TT
    J_NORM2 = J_XK + KT
    J_XV = J_NORM2 + 2 * TT
    J_XQ = J_XV + 2 * MT
    J_S = J_XQ + KT
    J_O = J_S + 4
    J_XO = J_O + KT
    J_NORM3 = J_XO + 2
    J_PQ = J_NORM3 + 2
    REST = SEQ - P
    NQ = 2 * PH
    J_SR = J_PQ + 2 * NQ
    J_OR = J_SR + 4 * (TT - 1)
    J_XOR = J_OR + KT
    J_NORM3R = J_XOR + 2 * (TT - 1)
    J_PQR = J_NORM3R + 2 * (TT - 1)
    G_S, G_O, G_N, G_PQ = 0, 1, 3, 4
    G_END = G_PQ + PH

    def job_s(i):
        return J_S if i == 0 else J_SR + 4 * (i - 1)

    def job_p(i):
        return job_s(i) + 2

    def job_f(c):
        return J_PQ + (2 * c - 1 if c else 0)

    def job_k(c):
        return J_PQ + (2 * c + 2 if c < NQ - 1 else 2 * NQ - 1)

    def job_fr(c):
        return J_PQR + 2 * (c - c % 2) + c % 2

    def job_kr(c):
        return job_fr(c) + 2

    def plain(w2, col, job):
        return [(w2, col + s, job + s) for s in range(RING)]

    def by_tokens(w2, col, job, tiles):
        return [(w2, col + s, job + tiles * (s // 4) + tiles - 1) for s in range(RING)]

    w_in2, wa2 = w_in[0], w_branch_attn[0]
    blocks = [plain(w_in2, COLQ, J_QK), plain(w_in2, COLK, J_QK + KT), by_tokens(w_in2, COLV, J_V, TT)]
    B_MIX = len(blocks)
    for m in range(0, KT, 2):
        blocks.append([(w_in2, (COLX, COLC, COLB, COLGC)[s % 4] + m + s // 4, J_MIX + 4 * m + s) for s in range(RING)])
    B_WC = len(blocks)
    blocks.append(plain(w_branch_conv[0], 0, J_WC))
    B_GA = len(blocks)
    for m in range(0, KT, 4):
        blocks.append([((w_in2, COLGA) if s % 2 == 0 else (wa2, 0)) for s in range(RING)])
        blocks[-1] = [(w2, c0 + m + s // 2, J_GA + 2 * m + s) for s, (w2, c0) in enumerate(blocks[-1])]
    B_WO = len(blocks)
    blocks.append(by_tokens(w_out[0], 0, J_WO, TT))
    B_XK = len(blocks)
    blocks.append(plain(xattn_wk[0], 0, J_XK))
    B_XV = len(blocks)
    blocks.append(by_tokens(xattn_wv[0], 0, J_XV, MT))
    B_XQ = len(blocks)
    blocks.append(plain(xattn_wq[0], 0, J_XQ))
    B_XO = len(blocks)
    blocks.append(by_tokens(xattn_wo[0], 0, J_XO, 1))
    B_PQ = len(blocks)
    for c in range(0, NQ, RING):
        blocks.append([(peer_w_query[0], c + s, job_f(c + s)) for s in range(RING)])
    HALF = RING // 2
    B_XOR = len(blocks)
    for half in range(2):
        blocks.append([None] * HALF + [(xattn_wo[0], 4 * half + s, J_XOR + (TT - 1) * half + TT - 2)
                                       for s in range(HALF)])
    B_PQR = len(blocks)
    for c in range(0, NQ, HALF):
        blocks.append([None] * HALF + [(peer_w_query[0], c + s, job_fr(c + s)) for s in range(HALF)])

    with ExitStack() as ctx:
        def sb(name, shape, dt=F32):
            return ctx.enter_context(nc.sbuf_tensor(name, shape, dt))

        def sem(name):
            return ctx.enter_context(nc.semaphore(name))

        def sb_both(name, shape):
            with nc.sbuf_tensor(name + "_r", shape, F32R) as rounded:
                pass
            return sb(name, shape), rounded

        xT, xT_r = sb_both("xT", [P, KT, SEQ])
        qk, qk_r = sb_both("qk", [P, 2 * KT, SEQ])
        vbuf, vbuf_r = sb_both("vbuf", [P, TT, D])
        h = sb("h", [P, TT, D])
        ymix, ymix_r = sb_both("ymix", [P, 2 * KT, SEQ])
        wring = sb("wring", [P, RING, KT, P])
        memkv, memkv_r = sb_both("memkv", [P, 4, D])
        keysT = sb("keysT", [P, NQ, NK])
        workf = sb("workf", [P, 9 * BANK])
        ident = sb("ident", [P, P])
        tri = sb("tri", [P, P], F32R)
        ones_r = sb("ones_r", [P, P], F32R)
        sp_hi = sb("sp_hi", [P, SPAN], F32R)
        sp_lo = sb("sp_lo", [P, SPAN], F32R)
        cmask = sb("cmask", [P, P])
        nmask = sb("nmask", [P, P])
        rows = sb("rows", [NROW, P])
        cols = sb("cols", [P, NROW])
        ms = sb("ms", [P, 4 * TT + MT])
        rms = sb("rms", [P, 4 * TT + MT])
        u_pad = sb("u_pad", [P, SEQ + CONVK - 1])
        cxs = sb("cxs", [P, SEQ])
        ytap = sb("ytap", [P, SEQ])
        neg_half = sb("neg_half", [P, 1])
        iota16 = sb("iota16", [P, TOPK])
        xmax = sb("xmax", [P, TT, XH])
        xneg = sb("xneg", [P, TT, XH])
        xsum = sb("xsum", [P, TT, XH])
        xinv = sb("xinv", [P, TT, XH])
        top_i = sb("top_i", [P, 2, TOPK], U32)
        best = sb("best", [P, 2, TOPK])
        pos = sb("pos", [P, TOPK], U32)
        pos_ab = sb("pos_ab", [P, 2, TOPK], U32)
        idx_u = sb("idx_u", [P, 2, TOPK], U32)
        idx_v = sb("idx_v", [P, 2, TOPK], U32)
        neg_best = sb("neg_best", [P, 2])
        gate_s = sb("gate_s", [P, 2])
        gate_r = sb("gate_r", [P, 2])

        jb = ctx.enter_context(nc.psum_tensor("jb", [P, BANKS, BANK], F32))
        ab = ctx.enter_context(nc.psum_tensor("ab", [P, 4, BANK], F32))

        qT, kT = qk[:, 0:KT, :], qk[:, KT:2 * KT, :]
        yconv, merged = ymix[:, 0:KT, :], ymix[:, KT:2 * KT, :]
        yflat = yconv.rearrange("p k t -> p (k t)")
        mem_tok = yflat[:, 0:MT * D].rearrange("p (i d) -> p i d", i=MT)
        keys_raw = vbuf[:, 0:2, :].rearrange("p a (c n) -> p (a c) n", n=P)
        xq_hi, xq_lo = ymix_r[:, 0:KT, :], ymix_r[:, KT:2 * KT, :]
        yc_hi, yc_lo = memkv_r[:, :, :].rearrange("p a (b t) -> p (a b) t", b=2), ymix_r[:, 0:KT, :]
        xg_hi, xg_lo = vbuf_r[:, :, :].rearrange("p a (b t) -> p (a b) t", b=2), xT_r
        ya_hi, ya_lo = qk_r[:, KT:2 * KT, :], qk_r[:, 0:KT, :]
        xc_hi, xc_lo = ymix_r[:, 0:KT, :], xT_r
        mg_hi, mg_lo = yc_hi, ymix_r[:, KT:2 * KT, :]
        mem_hi, mem_lo = (vbuf_r[:, 2 * n:2 * n + 2, :].rearrange("p a (b m) -> p (a b) m", m=M) for n in range(2))
        w_hi = sp_hi[:, 0:2 * BANK].rearrange("p (c k n) -> p c k n", c=2, k=KT // 2)
        w_lo = sp_lo[:, 0:2 * BANK].rearrange("p (c k n) -> p c k n", c=2, k=KT // 2)
        zs, spb, wbuf = (workf[:, 3 * BANK * n:3 * BANK * n + SPAN] for n in range(3))
        gex = workf[:, 6 * BANK:8 * BANK].rearrange("p (b t) -> p b t", b=2)
        ones = workf[:, 0:P]
        cur = cxs[:, 0:2 * NK].rearrange("p (c n) -> p c n", c=2)
        top_v, top_f, pos_f, sel, dots, wgt, gate_e = (
            ytap[:, 2 * TOPK * n:2 * TOPK * (n + 1)].rearrange("p (c k) -> p c k", c=2) for n in range(7))
        gl = ytap[:, 14 * TOPK:18 * TOPK].rearrange("p (c k) -> p c k", c=4)
        xnb = [workf[:, D * n:D * (n + 1)] for n in range(TT)]
        memT = workf[:, 2 * D:2 * D + KT * M].rearrange("p (k m) -> p k m", k=KT)
        diag = workf[:, 0:TOPK * P].rearrange("p (e n) -> p e n", e=TOPK)
        xcur = workf[:, 2 * D:3 * D]
        oT = qT
        q3 = workf[:, 3 * D:4 * D].rearrange("p (b t) -> p b t", b=2)
        cand = workf[:, 4 * D:4 * D + TOPK * TOPK]
        hot = workf[:, 4 * D + TOPK * TOPK:4 * D + 2 * TOPK * TOPK].rearrange("p (k s) -> p k s", k=TOPK)
        memf = memkv[:, :, :].rearrange("p a d -> p (a d)")
        memk = memf[:, 0:KT * M].rearrange("p (k m) -> p k m", k=KT)
        memv = memf[:, KT * M:KT * M + MT * D].rearrange("p (i d) -> p i d", i=MT)
        g_ffn = vbuf[:, TT - 1, :]
        g_fin = keysT[:, 0:KT, :].rearrange("p c n -> p (c n)")
        probs0T = kT[:, 0:2, :].rearrange("p k t -> p (k t)").rearrange("p (b h t) -> p b h t", b=MT, h=XH)
        probsRT = xT[:, :, P:SEQ].rearrange("p (b h) t -> p b h t", b=MT)
        probs_tok = workf[:, 3 * D:4 * D]
        qkf = qk[:, :, :].rearrange("p a t -> p (a t)")
        scores = qkf.rearrange("p (i a c n) -> p i a c n", i=TT, a=PH, c=2)
        scores_g = qkf.rearrange("p (g c n) -> p g c n", g=GROUPS, c=2)
        URING, VRING = 8, 4
        u_rows = ymix[:, :, :].rearrange("p a t -> p (a t)").rearrange("p (s d) -> p s d", s=URING)
        v_rows = wring[:, 0:VRING, :, :].rearrange("p s k n -> p s (k n)")

        bank_done = [sem(f"bank_done{b}") for b in range(BANKS)]
        bank_free = [sem(f"bank_free{b}") for b in range(BANKS)]
        w_ready = [sem(f"w_ready{s}") for s in range(RING)]
        x_in = [sem(f"x_in{i}") for i in range(TT)]
        par_in, keys_in, mem_in, gffn_in, gfin_in = (
            sem(n) for n in ("par_in", "keys_in", "mem_in", "gffn_in", "gfin_in"))
        consts = sem("consts")
        pads = sem("pads")
        cols_rdy = sem("cols_rdy")
        sq_done = sem("sq_done")
        eps_done = sem("eps_done")
        rms_done = sem("rms_done")
        xn_done = sem("xn_done")
        x3_done = sem("x3_done")
        z_done = sem("z_done")
        zs_done = sem("zs_done")
        zc_done = sem("zc_done")
        ez_done = sem("ez_done")
        ln_done = sem("ln_done")
        sp_done = sem("sp_done")
        spm_done = sem("spm_done")
        hi_done = sem("hi_done")
        lo_done = sem("lo_done")
        c_done = sem("c_done")
        arg_done = sem("arg_done")
        argm_done = sem("argm_done")
        wt_done = sem("wt_done")
        y_done = sem("y_done")
        y_out = sem("y_out")
        cu_done = sem("cu_done")
        gs_done = sem("gs_done")
        ga_done = sem("ga_done")
        xm_done = sem("xm_done")
        xp_done = sem("xp_done")
        h_done = sem("h_done")
        sc_out = sem("sc_out")
        tk = sem("tk")
        best_rdy = sem("best_rdy")
        idx_rdy = sem("idx_rdy")
        idx_cp = sem("idx_cp")
        slot_ok = sem("slot_ok")
        gate_rdy = sem("gate_rdy")
        u_ready = [sem(f"u_ready{s}") for s in range(URING)]
        v_ready = [sem(f"v_ready{s}") for s in range(VRING)]
        u_used = sem("u_used")
        v_free = sem("v_free")
        xc_done = sem("xc_done")
        gl_done = sem("gl_done")
        gle_done = sem("gle_done")
        wgt_rdy = sem("wgt_rdy")
        diag_rdy = sem("diag_rdy")
        acc_free = sem("acc_free")
        hadd = sem("hadd")
        fin_done = sem("fin_done")
        out_done = sem("out_done")

        whi_done = sem("whi_done")
        wlo_done = sem("wlo_done")
        w_part = sem("w_part")
        ahi_done = sem("ahi_done")
        alo_done = sem("alo_done")

        chunks = []

        def tile_chunks(job, blk, count):
            first = len(chunks)
            for n in range(count):
                for half in range(2):
                    chunks.append((blk + n // RING, slice(n % RING, n % RING + 1),
                                   slice(KT // 2 * half, KT // 2 * (half + 1)), job + n if half else None))
            return first

        def column_chunks(job, blk, tiles):
            first = len(chunks)
            for half in range(2):
                for k in range(KT):
                    chunks.append((blk, slice(4 * half, 4 * half + 4), slice(k, k + 1),
                                   job + tiles * (half + 1) - 1 if k == KT - 1 else None))
            return first

        C_QK = tile_chunks(J_QK, 0, 2 * KT)
        C_V = column_chunks(J_V, 2, TT)
        C_WC = tile_chunks(J_WC, B_WC, KT)
        C_GA = tile_chunks(J_GA, B_GA, 2 * KT)
        C_WO = column_chunks(J_WO, B_WO, TT)
        C_XK = tile_chunks(J_XK, B_XK, KT)
        C_XV = column_chunks(J_XV, B_XV, MT)
        C_XQ = tile_chunks(J_XQ, B_XQ, KT)

        def chunk_weights(c):
            _, slots, terms, _ = chunks[c]
            if slots.stop - slots.start == 1:
                return wring[:, slots.start, terms, :]
            return wring[:, slots, terms.start, :]

        def wait_chunk_used(eng, c):
            if chunks[c][3] is not None:
                wait_job(eng, chunks[c][3])
            else:
                eng.wait_ge(w_part, sum(closes is None for *_, closes in chunks[:c + 1]))

        A_WC = TT
        A_GA = A_WC + KT
        A_WO = A_GA + 2 * KT
        A_MEM = A_WO + KT
        A_XQ = A_MEM + MT
        A_END = A_XQ + TT

        block = ctx.enter_context(nc.Block())

        def wait_free(eng, job):
            if job >= BANKS:
                eng.wait_ge(bank_free[job % BANKS], job // BANKS)

        def wait_job(eng, job):
            eng.wait_ge(bank_done[job % BANKS], job // BANKS + 1)

        def wait_taken(eng, job):
            eng.wait_ge(bank_free[job % BANKS], job // BANKS + 1)

        def wait_all_taken(eng, upto):
            for job in range(upto - BANKS, upto):
                wait_taken(eng, job)

        @block.sync
        def _(sp):
            for i in range(TT):
                sp.dma_start(h[:, i, :], x[0, P * i:P * (i + 1), :]).then_inc(x_in[i], 16)
            for n, blk in enumerate(blocks):
                for s in range(HALF if n >= B_XOR else 0, RING):
                    w2, c, _ = blk[s]
                    if n:
                        wait_job(sp, blocks[n - 1][s][2])
                    sp.dma_start(wring[:, s, :, :],
                                 w2.rearrange("(k p) n -> p k n", p=P)[:, :, P * c:P * (c + 1)]).then_inc(w_ready[s], 16)
                if n == B_GA + 1:
                    wait_all_taken(sp, J_GA)
                    sp.dma_start(mem_tok, mem[0].rearrange("(i p) d -> p i d", p=P)).then_inc(mem_in, 16)
                if n == B_XO:
                    sp.dma_start(g_ffn, norm_ffn[0].partition_broadcast(P)).then_inc(gffn_in, 16)
            wait_job(sp, job_kr(NQ - 1))
            sp.dma_start(g_fin, norm_final.partition_broadcast(P)).then_inc(gfin_in, 16)
            for i in range(TT):
                sp.wait_ge(fin_done, i + 1)
                sp.dma_start(out[0, P * i:P * (i + 1), :], vbuf[:, i, :]).then_inc(out_done, 16)
            sp.wait_ge(out_done, 16 * TT)

        @block.gpsimd
        def _(pool):
            pool.memset(ident[:, :], 0.0).then_inc(consts, 1)
            pool.memset(ones[:, :], 1.0).then_inc(consts, 1)
            pool.memset(nmask[:, :], 0.0).then_inc(consts, 1)
            pool.memset(neg_half[:, :], -0.5).then_inc(consts, 1)
            pool.wait_ge(consts, 4)
            pool.affine_select(out=ident[:, :], in_=ident[:, :], compare_op=ALU.not_equal, fill=1.0, base=0,
                               pattern=[[-1, P]], channel_multiplier=1).then_inc(consts, 1)
            pool.affine_select(out=tri[:, :], in_=ones[:, :], compare_op=ALU.is_ge, fill=0.0, base=0,
                               pattern=[[-1, P]], channel_multiplier=1).then_inc(consts, 1)
            pool.affine_select(out=cmask[:, :], in_=ones[:, :], compare_op=ALU.is_gt, fill=0.0, base=0,
                               pattern=[[1, P]], channel_multiplier=-1).then_inc(consts, 1)
            pool.affine_select(out=nmask[:, :], in_=nmask[:, :], compare_op=ALU.is_gt, fill=-1.0e30, base=0,
                               pattern=[[1, P]], channel_multiplier=-1).then_inc(consts, 1)
            pool.tensor_copy(ones_r[:, :], ones[:, :]).then_inc(consts, 1)
            pool.iota(iota16[:, :], pattern=[[1, TOPK]], base=0, channel_multiplier=0,
                      allow_small_or_imprecise_dtypes=True).then_inc(consts, 1)

            def inverse_rms(lo, hi):
                for n in range(lo, hi):
                    pool.wait_ge(sq_done, n + 1)
                    pool.tensor_scalar(rms[:, n:n + 1], ms[:, n:n + 1], EPS, None, ALU.add).then_inc(eps_done, 1)
                    pool.wait_ge(eps_done, n + 1)
                    pool.tensor_tensor(rms[:, n:n + 1], rms[:, n:n + 1], neg_half[:, :],
                                       ALU.pow).then_inc(rms_done, 1)

            def gather(table, index, to, ready):
                pool.indirect_dma_start(out=to, out_offset=None, in_=table,
                                        in_offset=bass.IndirectOffsetOnAxis(ap=index, axis=0)).then_inc(ready, 16)

            inverse_rms(0, 2 * TT + MT + 1)
            pool.wait_ge(idx_rdy, 1)
            pool.sem_inc(acc_free, 2)
            for e in range(TOPK):
                if e >= URING:
                    pool.wait_ge(u_used, e - URING + 1)
                gather(peer_u[0], idx_u[:, 0, e:e + 1], u_rows[:, e % URING, :], u_ready[e % URING])
            wait_job(pool, job_f(NQ - 1))
            pool.sem_inc(v_free, VRING)

            def pair(i, last):
                for b in range(2):
                    with_u = not (last and b == 1)
                    pool.wait_ge(idx_rdy, i * 2 + (b + 1))
                    pool.sem_inc(slot_ok, 1)
                    pool.tensor_copy(idx_v[:, b, :], idx_u[:, b, :]).then_inc(idx_cp, 1)
                    pool.wait_ge(idx_cp, i * 2 + (b + 1))
                    pool.sem_inc(slot_ok, 1)
                    if with_u:
                        pool.wait_ge(idx_rdy, i * 2 + (b + 2))
                        pool.sem_inc(slot_ok, 1)
                    for e in range(TOPK):
                        if with_u:
                            pool.wait_ge(u_used, i * (2 * TOPK) + (TOPK * (b + 1) + e - URING + 1))
                            pool.sem_inc(slot_ok, 1)
                            gather(peer_u[0], idx_u[:, 1 - b, e:e + 1], u_rows[:, e % URING, :], u_ready[e % URING])
                        pool.wait_ge(v_free, i * (2 * TOPK) + (TOPK * b + e + 1))
                        pool.sem_inc(slot_ok, 1)
                        gather(peer_v[0], idx_v[:, b, e:e + 1], v_rows[:, e % VRING, :], v_ready[e % VRING])
                        if isinstance(i, int) and 2 * i + b == G_N and e == 5:
                            inverse_rms(2 * TT + MT + 1, 3 * TT + MT)

            for i in range(G_N // 2 + 1):
                pair(i, False)
            with pool.Fori(G_N // 2 + 1, PAIRS - 1) as i:
                pair(i, False)
            inverse_rms(3 * TT + MT, 4 * TT + MT - 1)
            pair(PAIRS - 1, True)
            inverse_rms(4 * TT + MT - 1, 4 * TT + MT)

        @block.tensor
        def _(pe):
            pe.wait_ge(consts, 9)

            def transposes(job, tiles):
                wait_free(pe, job)
                for n, t in enumerate(tiles):
                    mm = pe.transpose(jb[:, job % BANKS, P * n:P * (n + 1)], t, ident[:, :])
                mm.then_inc(bank_done[job % BANKS], 1)

            def norm_transposes(job, done, count, tiles, source):
                for i in range(tiles):
                    pe.wait_ge(done, count + i + 1)
                    for half in range(2):
                        transposes(job + 2 * i + half, [source(i)[:, P * k:P * (k + 1)]
                                                        for k in range(4 * half, 4 * half + 4)])

            def feature_job(job, blk, s, act, n, lo=0, hi=KT):
                if lo == 0:
                    pe.wait_ge(w_ready[s], 16 * (blk + 1))
                    wait_free(pe, job)
                for k in range(lo, hi):
                    mm = pe.matmul(jb[:, job % BANKS, 0:n], wring[:, s, k, :], act[:, k, :],
                                   start=(k == 0), stop=(k == KT - 1))
                if hi == KT:
                    mm.then_inc(bank_done[job % BANKS], 1)

            def three_passes(to, stationary, moving, first, last):
                (s_hi, s_lo), (m_hi, m_lo) = stationary, moving
                for p, (st, mv) in enumerate(((s_hi, m_hi), (s_hi, m_lo), (s_lo, m_hi))):
                    mm = pe.matmul(to, st, mv, start=(first and p == 0), stop=(last and p == 2))
                return mm

            def split_job(job, c, a_hi, a_lo, n=SEQ):
                wait_free(pe, job)
                for half in range(2):
                    pe.wait_ge(wlo_done, c + half + 1)
                    for k in range(KT // 2):
                        kk = KT // 2 * half + k
                        mm = three_passes(jb[:, job % BANKS, 0:n], (w_hi[:, half, k, :], w_lo[:, half, k, :]),
                                          (a_hi[:, kk, :], a_lo[:, kk, :]), kk == 0, kk == KT - 1)
                    mm.then_inc(bank_done[job % BANKS] if half else w_part, 1)

            def split_token_jobs(job, c, a_hi, a_lo, tiles, pieces=None):
                for half in range(2):
                    for k in range(KT):
                        n = c + KT * half + k
                        pe.wait_ge(wlo_done, n + 1)
                        if pieces is not None and half == 0:
                            pe.wait_ge(alo_done, pieces + k + 1)
                        for i in range(tiles):
                            j = job + tiles * half + i
                            if k == 0:
                                wait_free(pe, j)
                            t = slice(P * i, P * (i + 1))
                            mm = three_passes(jb[:, j % BANKS, :], (a_hi[:, k, t], a_lo[:, k, t]),
                                              (w_hi[:, n % 2, :, :], w_lo[:, n % 2, :, :]), k == 0, k == KT - 1)
                            if k == KT - 1:
                                mm.then_inc(bank_done[j % BANKS], 1)
                            elif i == tiles - 1:
                                mm.then_inc(w_part, 1)

            def token_jobs(job, blk, act, tiles):
                for half in range(2):
                    for s in range(4 * half, 4 * half + 4):
                        pe.wait_ge(w_ready[s], 16 * (blk + 1))
                    for i in range(tiles):
                        j = job + tiles * half + i
                        wait_free(pe, j)
                        for k in range(KT):
                            mm = pe.matmul(jb[:, j % BANKS, :], act[:, k, P * i:P * (i + 1)],
                                           wring[:, 4 * half:4 * half + 4, k, :],
                                           start=(k == 0), stop=(k == KT - 1))
                        mm.then_inc(bank_done[j % BANKS], 1)

            pe.wait_ge(par_in, 64)
            pe.transpose(jb[:, 0, 0:NROW], rows[:, :], ident[0:NROW, 0:NROW]).then_inc(bank_done[0], 1)
            norm_transposes(J_NORM1, xn_done, 0, TT, lambda i: xnb[i % 2])
            pe.wait_ge(keys_in, 16)
            for n in range(4):
                transposes(J_KEYS + n, [keys_raw[:, 4 * n + c, :] for c in range(4)])

            wait_all_taken(pe, J_KEYS)
            pe.wait_ge(alo_done, A_WC)
            for n in range(2 * KT):
                split_job(J_QK + n, C_QK + 2 * n, xq_hi, xq_lo)
            split_token_jobs(J_V, C_V, xq_hi, xq_lo, TT)
            wait_all_taken(pe, J_MIX)

            def ab_cols(j, lo, n):
                o = OFF[j] + lo
                return ab[:, o // BANK, o % BANK:o % BANK + n]

            def head_scores(hd):
                m, r = hd // 2, DH * (hd % 2)
                for t in range(TT):
                    mm = pe.matmul(ab_cols(t, 0, WID[t]), kT[r:r + DH, m, P * t:P * (t + 1)],
                                   qT[r:r + DH, m, P * t:SEQ], start=True, stop=True)
                mm.then_inc(z_done, 1)

            head_scores(0)
            for hd in range(SBH):
                m, b, r = hd // 2, hd % 2, DH * (hd % 2)
                j = J_MIX + 4 * m + 2 * b
                s = 4 * (m % 2) + 2 * b
                if hd == 0:
                    feature_job(j, B_MIX + m // 2, s, xT, SEQ)
                pe.wait_ge(lo_done, hd + 1)
                for t in range(TT):
                    for tt in range(t, TT):
                        for part in (sp_hi, sp_lo):
                            mm = pe.matmul(ab_cols(t, P * (tt - t), WID[tt]), (tri if tt == t else ones_r)[:, :],
                                           part[:, OFF[tt]:OFF[tt] + WID[tt]], start=(tt == t and part is sp_hi),
                                           stop=(tt == TT - 1 and part is sp_lo))
                mm.then_inc(c_done, 1)
                feature_job(j + 1, B_MIX + m // 2, s + 1, xT, SEQ, 0, 2)
                if hd + 1 < SBH:
                    pe.wait_ge(arg_done, hd + 1)
                    head_scores(hd + 1)
                feature_job(j + 1, B_MIX + m // 2, s + 1, xT, SEQ, 2, KT)
                pe.wait_ge(wt_done, hd + 1)
                if hd:
                    pe.wait_ge(y_out, hd)
                for t in range(TT):
                    mm = pe.matmul(ab[r:r + DH, 3, P * t:SEQ], vbuf[:, t, P * m + r:P * m + r + DH],
                                   wbuf[:, OFF[t]:OFF[t] + WID[t]], start=(t == 0), stop=(t == TT - 1))
                mm.then_inc(y_done, 1)
                if hd + 1 < SBH:
                    n = 2 * (hd + 1)
                    feature_job(J_MIX + n, B_MIX + n // RING, n % RING, xT, SEQ)

            pe.wait_ge(alo_done, A_GA)
            for m in range(KT):
                split_job(J_WC + m, C_WC + 2 * m, yc_hi, yc_lo)
            pe.wait_ge(alo_done, A_WO)
            for m in range(KT):
                split_job(J_GA + 2 * m, C_GA + 4 * m, xg_hi, xg_lo)
                split_job(J_GA + 2 * m + 1, C_GA + 4 * m + 2, ya_hi, ya_lo)
            norm_transposes(J_MEMT, xn_done, TT, MT, lambda i: xnb[i % 2])
            split_token_jobs(J_WO, C_WO, mg_hi, mg_lo, TT, A_WO)

            pe.wait_ge(alo_done, A_XQ)
            for m in range(KT):
                split_job(J_XK + m, C_XK + 2 * m, mem_hi, mem_lo, M)
            norm_transposes(J_NORM2, xn_done, TT + MT, TT, lambda i: xnb[i])
            split_token_jobs(J_XV, C_XV, mem_hi, mem_lo, MT)

            pe.wait_ge(alo_done, A_END)
            for m in range(KT):
                split_job(J_XQ + m, C_XQ + 2 * m, xc_hi, xc_lo)
            wait_all_taken(pe, J_S)

            def cross_scores(i, half):
                j = job_s(i) + half
                wait_free(pe, j)
                for hh in range(2):
                    for k in range(2):
                        kt = 2 * (2 * half + hh) + k
                        mm = pe.matmul(jb[:, j % BANKS, M * hh:M * (hh + 1)], qT[:, kt, P * i:P * (i + 1)],
                                       memk[:, kt, :], start=(k == 0), stop=(k == 1))
                mm.then_inc(bank_done[j % BANKS], 1)

            def cross_probs(i, src):
                pe.wait_ge(xp_done, 2 * (i + 1))
                for mb in range(MT):
                    transposes(job_p(i) + mb, [src[:, M * hx + P * mb:M * hx + P * (mb + 1)] for hx in range(XH)])

            def cross_output(j, m, probsT, n):
                wait_free(pe, j)
                for mb in range(MT):
                    mm = pe.matmul(jb[:, j % BANKS, 0:n], memv[:, mb, P * m:P * (m + 1)], probsT[:, mb, m // 2, :],
                                   start=(mb == 0), stop=(mb == MT - 1))
                mm.then_inc(bank_done[j % BANKS], 1)

            for half in range(2):
                cross_scores(0, half)
            cross_probs(0, xnb[0])
            wait_all_taken(pe, J_O)
            for m in range(KT):
                cross_output(J_O + m, m, probs0T, P)
            wait_all_taken(pe, J_XO)
            token_jobs(J_XO, B_XO, oT, 1)

            norm_transposes(J_NORM3, x3_done, 0, 1, lambda i: vbuf[:, i, :])
            wait_all_taken(pe, J_PQ)

            def key_scores(j, q_job, c, tiles):
                wait_free(pe, j)
                wait_taken(pe, q_job)
                for i in range(tiles):
                    mm = pe.matmul(jb[:, j % BANKS, P * (tiles - 1 - i):P * (tiles - i)],
                                   q3[:, c % 2, P * i:P * (i + 1)], keysT[:, c, :], start=True, stop=True)
                mm.then_inc(bank_done[j % BANKS], 1)

            for c in range(NQ):
                feature_job(job_f(c), B_PQ + c // RING, c % RING, xT[:, :, 0:P], P)
                if c:
                    key_scores(job_k(c - 1), job_f(c - 1), c - 1, 1)
            key_scores(job_k(NQ - 1), job_f(NQ - 1), NQ - 1, 1)

            def weighted_rows(i, b, chore=None):
                pe.wait_ge(acc_free, i * 2 + (b + 1))
                for e in range(TOPK):
                    pe.wait_ge(diag_rdy, i * (2 * TOPK) + (TOPK * b + e + 1))
                    pe.wait_ge(v_ready[e % VRING], i * (2 * TOPK // VRING * 16)
                               + 16 * (TOPK // VRING * b + e // VRING + 1))
                    for c in range(2):
                        mm = pe.matmul(ab[:, 2 * b + c, :], diag[:, e, :],
                                       v_rows[:, e % VRING, BANK * c:BANK * (c + 1)],
                                       start=(e == 0), stop=(e == TOPK - 1))
                    mm.then_inc(v_free, 1)
                    if chore:
                        chore(e)

            def rest_step(g, e):
                if g == G_S and e < 5 * (TT - 1):
                    i = 1 + e // 5
                    if e % 5 < 2:
                        cross_scores(i, e % 5)
                    elif e % 5 == 4:
                        cross_probs(i, probs_tok)
                elif g == G_O and e < 4:
                    if e == 0:
                        wait_all_taken(pe, J_OR)
                    for m in (2 * e, 2 * e + 1):
                        cross_output(J_OR + m, m, probsRT, REST)
                elif g in (G_O, G_O + 1) and e >= 4:
                    half, i, k0 = g - G_O, e // 4, 2 * (e % 4)
                    j = J_XOR + (TT - 1) * half + i - 1
                    if k0 == 0:
                        if g == G_O and i == 1:
                            wait_all_taken(pe, J_XOR)
                        if i == 1:
                            for s in range(HALF, RING):
                                pe.wait_ge(w_ready[s], 16 * (B_XOR + half + 1))
                        wait_free(pe, j)
                    for k in (k0, k0 + 1):
                        mm = pe.matmul(jb[:, j % BANKS, :], oT[:, k, P * i:P * (i + 1)], wring[:, HALF:RING, k, :],
                                       start=(k == 0), stop=(k == KT - 1))
                    if k == KT - 1:
                        mm.then_inc(bank_done[j % BANKS], 1)
                elif g == G_N and e >= 10:
                    i, half = 1 + (e - 10) // 2, e % 2
                    pe.wait_ge(x3_done, i + 1)
                    transposes(J_NORM3R + e - 10, [vbuf[:, i, P * k:P * (k + 1)] for k in range(4 * half, 4 * half + 4)])
                elif g >= G_PQ:
                    a = g - G_PQ
                    if a == 0 and e == 0:
                        wait_all_taken(pe, J_PQR)
                    if a and e < 2:
                        c = 2 * a - 2 + e
                        key_scores(job_kr(c), job_fr(c), c, TT - 1)
                    c, k = 2 * a + e // KT, e % KT
                    feature_job(job_fr(c), B_PQR + c // HALF, HALF + c % HALF, xT[:, :, P:SEQ], REST, k, k + 1)

            for g in range(G_END):
                weighted_rows(g // 2, g % 2, lambda e, g=g: rest_step(g, e))
            for c in (NQ - 2, NQ - 1):
                key_scores(job_kr(c), job_fr(c), c, TT - 1)
            with pe.Fori(G_END // 2, PAIRS) as i:
                for b in range(2):
                    weighted_rows(i, b)

        XSCALE = float(XD) ** -0.5

        def take_probs(act, i):
            for mb in range(MT):
                j = job_p(i) + mb
                wait_job(act, j)
                act.activation(probs0T[:, mb, :, :] if i == 0 else probsRT[:, mb, :, P * (i - 1):P * i],
                               jb[:, j % BANKS, :].rearrange("p (h t) -> p h t", h=XH),
                               ACT.Copy).then_inc(bank_free[j % BANKS], 1)

        def gate_exp(act, g, b):
            act.wait_ge(best_rdy, g + 1)
            act.activation(gate_e[:, b, :], best[:, b, :], ACT.Exp, bias=neg_best[:, b:b + 1],
                           accum_out=gate_s[:, b:b + 1]).then_inc(gate_rdy, 1)

        @block.scalar
        def _(act):
            for n, src in enumerate((norm_mix, norm_xattn, norm_mem)):
                act.dma_start(rows[KT * n:KT * (n + 1), :], src[0].rearrange("(k p) -> k p", p=P)).then_inc(par_in, 16)
            act.dma_start(rows[3 * KT:NROW, :], conv_w[0].rearrange("c (k p) -> (c k) p", p=P)).then_inc(par_in, 16)
            act.dma_start(keys_raw, peer_sub_keys[0].rearrange("h c n d -> n (h c) d")).then_inc(keys_in, 16)

            def mean_square(src, n, squares=ab[:, 2:4, :]):
                if n:
                    act.wait_ge(sq_done, n)
                act.activation(squares, src, ACT.Square,
                               scale=float(D) ** -0.5, accum_out=ms[:, n:n + 1]).then_inc(sq_done, 1)

            def normed(src, n, slot):
                act.wait_ge(rms_done, n + 1)
                act.activation(xnb[slot], src, ACT.Copy, scale=rms[:, n:n + 1]).then_inc(xn_done, 1)

            def high_part(src, to):
                act.activation(to, src, ACT.Copy).then_inc(ahi_done, 1)

            def high_weights(c, count=1):
                for n in range(c, c + count):
                    blk, slots, _, _ = chunks[n]
                    for slot in range(slots.start, slots.stop):
                        act.wait_ge(w_ready[slot], 16 * (blk + 1))
                    if n >= 2:
                        wait_chunk_used(act, n - 2)
                    act.activation(w_hi[:, n % 2, :, :], chunk_weights(n), ACT.Copy).then_inc(whi_done, 1)

            def x_high(i, job, to):
                for half in range(2):
                    wait_taken(act, job + 2 * i + half)
                high_part(xT[:, :, P * i:P * (i + 1)], to[:, :, P * i:P * (i + 1)])

            for i in range(TT):
                act.wait_ge(x_in[i], 16)
                mean_square(h[:, i, :], i)
                if i >= 2:
                    wait_job(act, J_NORM1 + 2 * (i - 2) + 1)
                normed(h[:, i, :], i, i % 2)
                if i:
                    x_high(i - 1, J_NORM1, xq_hi)
            high_weights(C_QK, 2)
            x_high(TT - 1, J_NORM1, xq_hi)

            def take(job, to, n=BANK, **kw):
                wait_job(act, job)
                act.activation(to, jb[:, job % BANKS, 0:n], kw.get("func", ACT.Copy),
                               scale=kw.get("scale", 1.0)).then_inc(bank_free[job % BANKS], 1)

            for n in range(2 * KT):
                high_weights(C_QK + 2 * n + 2, 2)
                take(J_QK + n, qk[:, n, :])
            high_weights(C_V + 2, KT - 1)
            for half in range(2):
                for i in range(TT):
                    take(J_V + TT * half + i, vbuf[:, i, BANK * half:BANK * (half + 1)])
                if half == 0:
                    high_weights(C_V + KT + 1, KT - 1)

            for hd in range(SBH + 1):
                m, b = hd // 2, hd % 2
                if hd < SBH:
                    act.wait_ge(zc_done, hd + 1)
                    act.activation(spb, spb, ACT.Exp).then_inc(ez_done, 1)
                    act.wait_ge(ez_done, hd + 1)
                    act.activation(spb, spb, ACT.Ln, bias=1.0).then_inc(ln_done, 1)
                if hd:
                    r = DH * (1 - b)
                    act.wait_ge(y_done, hd)
                    act.activation(qT[r:r + DH, (hd - 1) // 2, :], ab[r:r + DH, 3, :], ACT.Copy).then_inc(y_out, 1)
                    if b == 0:
                        take(J_MIX + 2 * hd - 1, merged[:, m - 1, :], func=ACT.Exp, scale=-1.0)
                if hd < SBH:
                    act.wait_ge(spm_done, hd + 1)
                    act.activation(sp_hi[:, :], spb, ACT.Copy).then_inc(hi_done, 1)
                    act.wait_ge(argm_done, hd + 1)
                    act.activation(wbuf, zs, ACT.Exp).then_inc(wt_done, 1)
                    if b == 0:
                        if m:
                            wait_taken(act, J_MIX + 4 * (m - 1) + 1)
                        take(J_MIX + 4 * m, cxs[:, :])
                        if m:
                            wait_taken(act, J_MIX + 4 * (m - 1) + 2)
                            high_part(yconv[:, m - 1, :], yc_hi[:, m - 1, :])

            high_weights(C_WC, 2)
            wait_taken(act, J_MIX + 4 * (KT - 1) + 2)
            high_part(yconv[:, KT - 1, :], yc_hi[:, KT - 1, :])
            for m in range(KT):
                high_weights(C_WC + 2 * m + 2, 2)
                high_part(xT[:, m, :], xg_hi[:, m, :])
                high_part(qT[:, m, :], ya_hi[:, m, :])
            for m in range(KT):
                high_weights(C_GA + 4 * m + 2, 2)
                if m >= 2:
                    act.wait_ge(ga_done, 3 * (m - 1))
                take(J_GA + 2 * m, gex[:, m % 2, :], func=ACT.Exp, scale=-1.0)
                high_weights(C_GA + 4 * m + 4, 2)
                if m:
                    act.wait_ge(ga_done, 3 * m)
                    high_part(merged[:, m - 1, :], mg_hi[:, m - 1, :])
                if m >= KT - MT:
                    i = m - (KT - MT)
                    act.wait_ge(mem_in, 16)
                    mean_square(mem_tok[:, i, :], TT + i)
                    normed(mem_tok[:, i, :], TT + i, i % 2)
            act.wait_ge(ga_done, 3 * KT)
            high_part(merged[:, KT - 1, :], mg_hi[:, KT - 1, :])
            high_weights(C_WO + 2, 2)
            for i in range(MT):
                for half in range(2):
                    wait_taken(act, J_MEMT + 2 * i + half)
                high_part(memT[:, :, P * i:P * (i + 1)], mem_hi[:, :, P * i:P * (i + 1)])
            high_weights(C_WO + 4, 2 * KT - 2)
            for m in range(KT):
                high_weights(C_XK + 2 * m + 2, 2)
                take(J_XK + m, memk[:, m, :], n=M)
                if m < TT:
                    wait_taken(act, J_WO + TT + m)
                    mean_square(h[:, m, :], TT + MT + m)
                    normed(h[:, m, :], TT + MT + m, m)
            for half in range(2):
                for n in range(KT - 1):
                    high_weights(C_XV + KT * half + 2 + n - half)
                    if half == 0 and n % 2 and n // 2 < TT - 1:
                        x_high(n // 2, J_NORM2, xc_hi)
                if half:
                    high_weights(C_XQ)
                for i in range(MT):
                    take(J_XV + MT * half + i, memv[:, i, BANK * half:BANK * (half + 1)])
            high_weights(C_XQ + 1)
            x_high(TT - 1, J_NORM2, xc_hi)
            for m in range(KT):
                if m + 1 < KT:
                    high_weights(C_XQ + 2 * m + 2, 2)
                take(J_XQ + m, qT[:, m, :])

            def exp_scores(i, to):
                act.wait_ge(xm_done, 2 * (i + 1))
                wait_job(act, job_p(i - 1) + 1 if i else J_XQ - 1)
                for hx in range(XH):
                    j = job_s(i) + hx // 2
                    ex = act.activation(to[:, M * hx:M * (hx + 1)],
                                        jb[:, j % BANKS, M * (hx % 2):M * (hx % 2 + 1)], ACT.Exp,
                                        scale=XSCALE, bias=xneg[:, i, hx:hx + 1], accum_out=xsum[:, i, hx:hx + 1])
                    if hx % 2:
                        ex.then_inc(bank_free[j % BANKS], 1)

            exp_scores(0, xnb[0])
            take_probs(act, 0)
            for m in range(KT):
                take(J_O + m, oT[:, m, 0:P], n=P)
            wait_taken(act, J_XO + 1)
            mean_square(h[:, 0, :], 2 * TT + MT)

            def take_key_scores(j, c, lo, hi, scored):
                wait_job(act, j)
                act.activation(scores[:, TT - hi:TT - lo, PH - 1 - c // 2, c % 2, :],
                               jb[:, j % BANKS, 0:P * (hi - lo)].rearrange("p (i n) -> p i n", i=hi - lo),
                               ACT.Copy).then_inc(bank_free[j % BANKS], 1)
                wait_taken(act, j)
                act.sem_inc(sc_out, scored)

            for c in range(NQ):
                if c >= 2:
                    wait_job(act, job_k(c - 2))
                take(job_f(c), q3[:, c % 2, 0:P], n=P)
                if c:
                    take_key_scores(job_k(c - 1), c - 1, 0, 1, 1)
                if c in (6, 10):
                    gate_exp(act, (c - 6) // 4, (c - 6) // 4)
            take_key_scores(job_k(NQ - 1), NQ - 1, 0, 1, 1)

            def take_rest(g):
                if g == G_S:
                    for i in range(1, TT):
                        exp_scores(i, probs_tok)
                        take_probs(act, i)
                elif g == G_O:
                    for m in range(KT):
                        take(J_OR + m, oT[:, m, P:SEQ], n=REST)
                elif g == G_N:
                    for i in range(1, TT):
                        wait_taken(act, J_XOR + TT - 1 + i - 1)
                        mean_square(h[:, i, :], 2 * TT + MT + i, sp_hi[:, 0:D])
                elif g >= G_PQ:
                    if g > G_PQ:
                        take_rest_scores(g - G_PQ - 1)
                    if g < G_END:
                        take_rest_queries(g - G_PQ)

            def take_rest_scores(g):
                for c in (2 * g, 2 * g + 1):
                    take_key_scores(job_kr(c), c, 1, TT, 1 if c < NQ - 1 else 2 * GROUPS - 2 * NQ + 1)

            def take_rest_queries(g):
                for c in (2 * g, 2 * g + 1):
                    wait_job(act, job_kr(c - 2) if g else job_k(NQ - 2 + c))
                    take(job_fr(c), q3[:, c % 2, 0:REST], n=REST)

            def pair(i, first, last):
                for b in range(2):
                    act.wait_ge(gl_done, i * 16 + (8 * b + 4))
                    act.activation(gl[:, 2, :], gl[:, 1, :], ACT.Exp, scale=-GELU_C).then_inc(gle_done, 1)
                    act.wait_ge(wgt_rdy, i * 2 + (b + 1))
                    for e in range(TOPK):
                        if not (first and b == 0):
                            act.wait_ge(v_free, i * (2 * TOPK) + (TOPK * (b - 1) + e + 1 + VRING))
                        act.activation(diag[:, e, :], ident[:, :], ACT.Copy,
                                       scale=wgt[:, b, e:e + 1]).then_inc(diag_rdy, 1)
                    if isinstance(i, int) and 2 * i + b < G_END:
                        take_rest(2 * i + b)
                    if not last:
                        gate_exp(act, i * 2 + (b + 2), b)

            for i in range(G_END // 2):
                pair(i, i == 0, False)
            take_rest(G_END)
            with act.Fori(G_END // 2, PAIRS - 1) as i:
                pair(i, False, False)
            for i in range(TT - 1):
                act.wait_ge(acc_free, 2 + PH * (i + 1))
                mean_square(h[:, i, :], 3 * TT + MT + i, sp_hi[:, 0:D])
            pair(PAIRS - 1, False, True)
            act.wait_ge(hadd, 1)
            mean_square(h[:, TT - 1, :], 4 * TT + MT - 1, sp_hi[:, 0:D])

        @block.vector
        def _(dve):
            dve.memset(u_pad[:, :], 0.0).then_inc(pads, 1)

            wait_job(dve, J_PARAM)
            dve.tensor_copy(cols[:, :], jb[:, 0, 0:NROW]).then_inc(bank_free[0], 1)
            wait_taken(dve, J_PARAM)

            def take_normed(job, i, to, g0):
                for half in range(2):
                    j = job + 2 * i + half
                    wait_job(dve, j)
                    src = jb[:, j % BANKS, :].rearrange("p (k t) -> p k t", k=4)
                    dst = to[:, 4 * half:4 * half + 4, P * i:P * (i + 1)]
                    if g0 is None:
                        dve.tensor_copy(dst, src).then_inc(bank_free[j % BANKS], 1)
                    else:
                        gain = cols[:, g0 + 4 * half:g0 + 4 * half + 4].unsqueeze(2).to_broadcast([P, 4, P])
                        dve.tensor_tensor(dst, src, gain, ALU.mult).then_inc(bank_free[j % BANKS], 1)

            def low_part(n, src, high, to):
                dve.wait_ge(ahi_done, n + 1)
                dve.tensor_tensor(to, src, high, ALU.subtract).then_inc(alo_done, 1)

            def low_weights(c, count=1):
                for n in range(c, c + count):
                    dve.wait_ge(whi_done, n + 1)
                    dve.tensor_tensor(w_lo[:, n % 2, :, :], chunk_weights(n), w_hi[:, n % 2, :, :],
                                      ALU.subtract).then_inc(wlo_done, 1)

            def x_low(n, i, hi, lo):
                t = slice(P * i, P * (i + 1))
                low_part(n, xT[:, :, t], hi[:, :, t], lo[:, :, t])

            for i in range(TT + 1):
                if i < TT:
                    take_normed(J_NORM1, i, xT, 0)
                if i:
                    if i == TT:
                        low_weights(C_QK, 2)
                    x_low(i - 1, i - 1, xq_hi, xq_lo)
            for n in range(4):
                j = J_KEYS + n
                wait_job(dve, j)
                dve.tensor_copy(keysT[:, 4 * n:4 * n + 4, :],
                                jb[:, j % BANKS, :].rearrange("p (c n) -> p c n", c=4)).then_inc(bank_free[j % BANKS], 1)
            dve.memset(zs[:, OFF[1] + WID[1]:OFF[2]], 0.0).then_inc(pads, 1)
            dve.memset(spb[:, OFF[1] + WID[1]:OFF[2]], 0.0).then_inc(pads, 1)
            dve.wait_ge(pads, 3)
            low_weights(C_QK + 2, C_WC - 2)

            z_parts = [(ab[:, 0, :], lambda t: t[:, 0:BANK]),
                       (ab[:, 1, 0:WID[1]], lambda t: t[:, OFF[1]:OFF[1] + WID[1]]),
                       (ab[:, 2, 0:WID[1]], lambda t: t[:, OFF[2]:OFF[2] + WID[1]])]

            def diagonal(t, op, mask, done):
                for n in range(TT):
                    d = t[:, OFF[n]:OFF[n] + P]
                    last = dve.tensor_tensor(d, d, mask[:, :], op)
                last.then_inc(done, 1)

            def sigmoid_tail(m):
                wait_taken(dve, J_MIX + 4 * m + 3)
                dve.tensor_scalar(merged[:, m, :], merged[:, m, :], 1.0, None, ALU.add).then_inc(gs_done, 1)
                dve.wait_ge(gs_done, 2 * m + 1)
                dve.reciprocal(merged[:, m, :], merged[:, m, :]).then_inc(gs_done, 1)

            def convolve(m):
                j = J_MIX + 4 * m + 1
                wait_job(dve, j)
                wait_taken(dve, j - 1)
                dve.tensor_tensor(u_pad[:, CONVK - 1:], jb[:, j % BANKS, :], cxs[:, :],
                                  ALU.mult).then_inc(bank_free[j % BANKS], 1)
                wait_taken(dve, j)
                for c in range(CONVK):
                    tap = cols[:, KT * (3 + c) + m:KT * (3 + c) + m + 1]
                    if c == 0:
                        if m:
                            wait_taken(dve, J_MIX + 4 * (m - 1) + 2)
                        st = dve.tensor_scalar(ytap[:, :], u_pad[:, 0:SEQ], tap, None, ALU.mult)
                    else:
                        dve.wait_ge(cu_done, 3 * m + c)
                        st = dve.scalar_tensor_tensor(out=ytap[:, :], in0=u_pad[:, c:c + SEQ], scalar=tap,
                                                      in1=ytap[:, :], op0=ALU.mult, op1=ALU.add)
                    st.then_inc(cu_done, 1)

            def gate_convolved(m):
                j = J_MIX + 4 * m + 2
                wait_job(dve, j)
                dve.wait_ge(cu_done, 3 * (m + 1))
                dve.tensor_tensor(yconv[:, m, :], jb[:, j % BANKS, :], ytap[:, :],
                                  ALU.mult).then_inc(bank_free[j % BANKS], 1)

            for hd in range(SBH):
                m, b = hd // 2, hd % 2
                dve.wait_ge(z_done, hd + 1)
                if hd:
                    dve.wait_ge(wt_done, hd)
                for ps, part in z_parts:
                    last = dve.tensor_scalar(part(zs), ps, float(DH) ** -0.5, None, ALU.mult)
                last.then_inc(zs_done, 1)
                dve.wait_ge(zs_done, hd + 1)
                dve.tensor_scalar(spb, zs, SP_CAP, None, ALU.min).then_inc(zc_done, 1)
                if m and b:
                    sigmoid_tail(m - 1)
                    low_part(A_WC + m - 1, yconv[:, m - 1, :], yc_hi[:, m - 1, :], yc_lo[:, m - 1, :])
                elif m:
                    convolve(m - 1)
                dve.wait_ge(ln_done, hd + 1)
                dve.tensor_tensor(spb, spb, zs, ALU.max).then_inc(sp_done, 1)
                dve.wait_ge(sp_done, hd + 1)
                diagonal(spb, ALU.mult, cmask, spm_done)
                dve.wait_ge(hi_done, hd + 1)
                dve.tensor_tensor(sp_lo[:, :], spb, sp_hi[:, :], ALU.subtract).then_inc(lo_done, 1)
                dve.wait_ge(c_done, hd + 1)
                for ps, part in z_parts:
                    last = dve.tensor_tensor(part(zs), part(zs), ps, ALU.subtract)
                last.then_inc(arg_done, 1)
                dve.wait_ge(arg_done, hd + 1)
                diagonal(zs, ALU.min, nmask, argm_done)
                if m and b == 0:
                    gate_convolved(m - 1)
            convolve(KT - 1)
            gate_convolved(KT - 1)
            low_weights(C_WC, 2)
            low_part(A_WC + KT - 1, yconv[:, KT - 1, :], yc_hi[:, KT - 1, :], yc_lo[:, KT - 1, :])
            sigmoid_tail(KT - 1)

            for m in range(KT):
                j = J_WC + m
                low_weights(C_WC + 2 * m + 2, 2)
                low_part(A_GA + 2 * m, xT[:, m, :], xg_hi[:, m, :], xg_lo[:, m, :])
                low_part(A_GA + 2 * m + 1, qT[:, m, :], ya_hi[:, m, :], ya_lo[:, m, :])
                wait_job(dve, j)
                dve.wait_ge(gs_done, 2 * (m + 1))
                dve.tensor_tensor(merged[:, m, :], jb[:, j % BANKS, :], merged[:, m, :],
                                  ALU.mult).then_inc(bank_free[j % BANKS], 1)
            for m in range(KT):
                j = J_GA + 2 * m
                gx = gex[:, m % 2, :]
                low_weights(C_GA + 4 * m + 2, 2)
                wait_taken(dve, j)
                dve.tensor_scalar(gx, gx, 1.0, None, ALU.add).then_inc(ga_done, 1)
                dve.wait_ge(ga_done, 3 * m + 1)
                dve.reciprocal(gx, gx).then_inc(ga_done, 1)
                low_weights(C_GA + 4 * m + 4, 2)
                if m:
                    low_part(A_WO + m - 1, merged[:, m - 1, :], mg_hi[:, m - 1, :], mg_lo[:, m - 1, :])
                dve.wait_ge(ga_done, 3 * m + 2)
                wait_job(dve, j + 1)
                dve.tensor_tensor(gx, jb[:, (j + 1) % BANKS, :], gx, ALU.mult).then_inc(bank_free[(j + 1) % BANKS], 1)
                wait_taken(dve, j + 1)
                wait_taken(dve, J_WC + m)
                dve.tensor_tensor(merged[:, m, :], merged[:, m, :], gx, ALU.add).then_inc(ga_done, 1)

            low_part(A_WO + KT - 1, merged[:, KT - 1, :], mg_hi[:, KT - 1, :], mg_lo[:, KT - 1, :])
            for i in range(MT):
                take_normed(J_MEMT, i, memT, 2 * KT)
            low_weights(C_WO + 2, 2)
            for i in range(MT):
                t = slice(P * i, P * (i + 1))
                low_part(A_MEM + i, memT[:, :, t], mem_hi[:, :, t], mem_lo[:, :, t])
            low_weights(C_WO + 4, KT - 4)

            for half in range(2):
                low_weights(C_WO + KT * (half + 1))
                for i in range(TT):
                    j = J_WO + TT * half + i
                    wait_job(dve, j)
                    hh = h[:, i, BANK * half:BANK * (half + 1)]
                    dve.tensor_tensor(hh, jb[:, j % BANKS, :], hh, ALU.add).then_inc(bank_free[j % BANKS], 1)
                if half == 0:
                    low_weights(C_WO + KT + 1, KT - 1)
            low_weights(C_XK + 1, 2 * KT + 1)
            for i in range(TT):
                take_normed(J_NORM2, i, xT, KT)
            for n in range(C_XV + 2, C_XQ + 2):
                low_weights(n)
                if (n - C_XV) % 2 and n - C_XV < 2 * TT:
                    x_low(A_XQ + (n - C_XV) // 2 - 1, (n - C_XV) // 2 - 1, xc_hi, xc_lo)
            x_low(A_XQ + TT - 1, TT - 1, xc_hi, xc_lo)
            low_weights(C_XQ + 2, 2 * KT - 2)

            def row_maxima(i):
                for half in range(2):
                    j = job_s(i) + half
                    wait_job(dve, j)
                    rd = dve.tensor_reduce(xmax[:, i, 2 * half:2 * half + 2],
                                           jb[:, j % BANKS, :].rearrange("p (h m) -> p h m", h=2), AX.X, ALU.max)
                rd.then_inc(xm_done, 1)
                dve.wait_ge(xm_done, 2 * i + 1)
                dve.tensor_scalar(xneg[:, i, :], xmax[:, i, :], -XSCALE, None, ALU.mult).then_inc(xm_done, 1)

            def probabilities(i, tok):
                for half in range(2):
                    wait_taken(dve, job_s(i) + half)
                dve.reciprocal(xinv[:, i, :], xsum[:, i, :]).then_inc(xp_done, 1)
                dve.wait_ge(xp_done, 2 * i + 1)
                pr = tok.rearrange("p (h m) -> p h m", h=XH)
                dve.tensor_tensor(pr, pr, xinv[:, i, :].unsqueeze(2).to_broadcast([P, XH, M]),
                                  ALU.mult).then_inc(xp_done, 1)

            def add_output(j, i, half):
                wait_job(dve, j)
                hh = h[:, i, BANK * half:BANK * (half + 1)]
                dve.tensor_tensor(hh, jb[:, j % BANKS, :], hh, ALU.add).then_inc(bank_free[j % BANKS], 1)

            def norm_tile(i):
                n = 2 * TT + MT + i
                dve.wait_ge(rms_done, n + 1)
                dve.scalar_tensor_tensor(out=vbuf[:, i, :], in0=h[:, i, :], scalar=rms[:, n:n + 1], in1=g_ffn,
                                         op0=ALU.mult, op1=ALU.mult).then_inc(x3_done, 1)

            row_maxima(0)
            probabilities(0, xnb[0])
            for half in range(2):
                add_output(J_XO + half, 0, half)
            dve.wait_ge(gffn_in, 16)
            norm_tile(0)
            take_normed(J_NORM3, 0, xT, None)

            def rest_step(g, e):
                if g == G_S and e < 5 * (TT - 1):
                    if e % 5 == 1:
                        row_maxima(1 + e // 5)
                    elif e % 5 == 2:
                        probabilities(1 + e // 5, probs_tok)
                if g in (G_O, G_O + 1) and e in (9, 13) or g in (G_O + 1, G_O + 2) and e == 1:
                    n = (e - 9) // 4 if e > 1 else 2
                    half = g - G_O - (e == 1)
                    add_output(J_XOR + (TT - 1) * half + n, 1 + n, half)
                if g == G_N and e in (8, 9, 10):
                    norm_tile(e - 7)
                if g == G_N and e >= 13:
                    take_normed(J_NORM3R, e - 13, xT[:, :, P:SEQ], None)

            def select(g, b):
                n = [0]

                def after(ins):
                    ins.then_inc(tk, 1)
                    n[0] += 1
                    dve.wait_ge(tk, n[0])

                def top16(vals, src, where):
                    after(dve.max(vals[:, 0:8], src))
                    after(dve.max_index(where[:, 0:8], vals[:, 0:8], src))
                    after(dve.match_replace(src, vals[:, 0:8], src, LOWEST))
                    after(dve.max(vals[:, 8:16], src))
                    after(dve.max_index(where[:, 8:16], vals[:, 8:16], src))

                dve.wait_ge(sc_out, g * 2 + 2)
                after(dve.tensor_copy(cur[:, :, :], scores_g[:, GROUPS - 1 - g, :, :] if isinstance(g, int)
                                      else scores_g[:, bass.ds(g * -1 + (GROUPS - 1), 1), :, :]
                                      .rearrange("p g c n -> p (g c) n")))
                for c in range(2):
                    top16(top_v[:, c, :], cur[:, c, :], top_i[:, c, :])
                candv = cand.rearrange("p (a b) -> p a b", a=TOPK)
                after(dve.tensor_tensor(candv, top_v[:, 0, :].unsqueeze(2).to_broadcast([P, TOPK, TOPK]),
                                        top_v[:, 1, :].unsqueeze(1).to_broadcast([P, TOPK, TOPK]), ALU.add))
                after(dve.tensor_scalar(top_f[:, 0, :], top_i[:, 0, :], float(NK), None, ALU.mult))
                after(dve.tensor_copy(top_f[:, 1, :], top_i[:, 1, :]))
                top16(best[:, b, :], cand, pos[:, :])
                dve.tensor_scalar(neg_best[:, b:b + 1], best[:, b, 0:1], -1.0, None, ALU.mult).then_inc(best_rdy, 1)
                after(dve.tensor_scalar(pos_ab[:, 0, :], pos[:, :], 4, None, ALU.logical_shift_right))
                after(dve.tensor_scalar(pos_ab[:, 1, :], pos[:, :], TOPK - 1, None, ALU.bitwise_and))
                after(dve.tensor_copy(pos_f[:, :, :], pos_ab[:, :, :]))
                for c in range(2):
                    after(dve.tensor_tensor(hot, pos_f[:, c, :].unsqueeze(2).to_broadcast([P, TOPK, TOPK]),
                                            iota16[:, :].unsqueeze(1).to_broadcast([P, TOPK, TOPK]), ALU.is_equal))
                    after(dve.tensor_tensor(hot, hot, top_f[:, c, :].unsqueeze(1).to_broadcast([P, TOPK, TOPK]),
                                            ALU.mult))
                    after(dve.tensor_reduce(sel[:, c, :], hot, AX.X, ALU.add))
                dve.sem_clear(tk)
                dve.tensor_tensor(idx_u[:, b, :], sel[:, 0, :], sel[:, 1, :], ALU.add).then_inc(idx_rdy, 1)

            dve.wait_ge(consts, 10)
            select(0, 0)
            select(1, 1)

            def tile_of(t, q):
                return t[:, q, :] if isinstance(q, int) else t[:, bass.ds(q, 1), :].rearrange("p a d -> p (a d)")

            def add_experts(i, b):
                dve.wait_ge(v_free, i * (2 * TOPK) + (TOPK * (b + 1) + VRING))
                hh = tile_of(h, i // (PH // 2))
                return dve.tensor_tensor(hh, ab[:, 2 * b:2 * b + 2, :].rearrange("p c n -> p (c n)"), hh, ALU.add)

            def final_norm(i):
                n = 3 * TT + MT + i
                dve.wait_ge(rms_done, n + 1)
                dve.scalar_tensor_tensor(out=vbuf[:, i, :], in0=h[:, i, :], scalar=rms[:, n:n + 1], in1=g_fin,
                                         op0=ALU.mult, op1=ALU.mult).then_inc(fin_done, 1)

            def pair(i, first, last):
                for b in range(2):
                    if last and b == 1:
                        dve.wait_ge(gfin_in, 16)
                        for t in range(TT - 1):
                            final_norm(t)
                    if b == 0:
                        dve.tensor_copy(xcur, tile_of(vbuf, i // (PH // 2))).then_inc(xc_done, 1)
                        dve.wait_ge(xc_done, i + 1)
                    for e in range(TOPK):
                        dve.wait_ge(u_ready[e % URING], i * (2 * TOPK // URING * 16)
                                    + 16 * (TOPK // URING * b + e // URING + 1))
                        u = u_rows[:, e % URING, :]
                        dve.tensor_tensor_reduce(out=u, in0=u, in1=xcur, scale=1.0, scalar=0.0, op0=ALU.mult,
                                                 op1=ALU.add, accum_out=dots[:, b, e:e + 1]).then_inc(u_used, 1)
                        if isinstance(i, int) and i + b > 0:
                            rest_step(2 * i + b - 1, e)
                    a = dots[:, b, :]
                    n = [0]

                    def step(ins):
                        ins.then_inc(gl_done, 1)
                        n[0] += 1

                    def wait_steps():
                        dve.wait_ge(gl_done, i * 16 + (8 * b + n[0]))

                    dve.wait_ge(u_used, i * (2 * TOPK) + TOPK * (b + 1))
                    step(dve.tensor_tensor(gl[:, 0, :], a, a, ALU.mult))
                    wait_steps()
                    step(dve.tensor_scalar(gl[:, 0, :], gl[:, 0, :], 0.044715, 1.0, ALU.mult, ALU.add))
                    wait_steps()
                    step(dve.tensor_tensor(gl[:, 1, :], gl[:, 0, :], a, ALU.mult))
                    wait_steps()
                    step(dve.tensor_scalar(gl[:, 1, :], gl[:, 1, :], GELU_FLOOR, None, ALU.max))
                    dve.wait_ge(gate_rdy, i * 2 + (b + 1))
                    step(dve.tensor_tensor(gl[:, 3, :], a, gate_e[:, b, :], ALU.mult))
                    step(dve.reciprocal(gate_r[:, b:b + 1], gate_s[:, b:b + 1]))
                    dve.wait_ge(gle_done, i * 2 + (b + 1))
                    step(dve.tensor_scalar(gl[:, 2, :], gl[:, 2, :], 1.0, None, ALU.add))
                    wait_steps()
                    step(dve.reciprocal(gl[:, 2, :], gl[:, 2, :]))
                    wait_steps()
                    if not first:
                        dve.wait_ge(diag_rdy, i * (2 * TOPK) + TOPK * (b - 1))
                    dve.scalar_tensor_tensor(out=wgt[:, b, :], in0=gl[:, 3, :], scalar=gate_r[:, b:b + 1],
                                             in1=gl[:, 2, :], op0=ALU.mult, op1=ALU.mult).then_inc(wgt_rdy, 1)
                    if not last:
                        dve.wait_ge(idx_cp, i * 2 + (b + 1))
                        select(i * 2 + (b + 2), b)
                    if not (first and b == 0):
                        add_experts(i - (1 - b), 1 - b).then_inc(acc_free, 1)

            for i in range(G_N // 2 + 2):
                pair(i, i == 0, False)
            with dve.Fori(G_N // 2 + 2, PAIRS - 1) as i:
                pair(i, False, False)
            pair(PAIRS - 1, False, True)
            dve.wait_ge(acc_free, 2 * PAIRS + 1)
            add_experts(PAIRS - 1, 1).then_inc(hadd, 1)

            final_norm(TT - 1)


_INS = ["x", "mem", "norm_mix", "w_in", "conv_w", "w_branch_attn", "w_branch_conv", "w_out", "norm_xattn", "norm_mem",
        "xattn_wq", "xattn_wk", "xattn_wv", "xattn_wo", "norm_ffn", "peer_w_query", "peer_sub_keys", "peer_u",
        "peer_v", "norm_final"]


def kernel(**inputs):
    import numpy as _np
    import concourse.bacc as _bacc
    from concourse import mybir as _mybir
    from concourse.bass_utils import run_bass_kernel_spmd as _run

    nc = _bacc.Bacc("TRN2", target_bir_lowering=False, num_devices=1)
    arrays, args = {}, []
    for name in _INS:
        a = _np.ascontiguousarray(inputs[name])
        arrays[f"in_{name}_dram"] = a
        args.append(nc.dram_tensor(f"in_{name}_dram", a.shape, _mybir.dt.from_np(a.dtype), kind="ExternalInput").ap())
    shape = inputs["x"].shape
    args.append(nc.dram_tensor("out_0_dram", shape, _mybir.dt.float32, kind="ExternalOutput").ap())
    build_trunk(nc, *args)
    r = _run(nc, [arrays], core_ids=[0])
    return r.results[0]["out_0_dram"]
```
